# Optimizing a Trainium2 kernel written in Bass

```python
import math
import jax, jax.numpy as jnp
from jax import lax
import numpy as np

D_MODEL = 1024
BATCH = 1
SEQ = 1024
DEPTH = 1

CHUNK = 64
POOL_WIDTH = D_MODEL // 2
POOL_WINDOWS = (2, 4, 8, 16)
N_POOL_GROUPS = len(POOL_WINDOWS)
POOL_GROUP = POOL_WIDTH // N_POOL_GROUPS
ATTN_WIDTH = D_MODEL - POOL_WIDTH
HEAD_DIM = 64
N_HEADS = ATTN_WIDTH // HEAD_DIM
Q_BLOCK = 128
IN_WIDTH = POOL_WIDTH + 3 * ATTN_WIDTH + N_HEADS
N_EXPERTS = 32
TOP_K = 4
D_EXPERT = D_MODEL
SWIGLU_LIMIT = 7.0
SWIGLU_ALPHA = 1.702
EXPERT_BLOCK = 128
RMS_EPS = 1e-5

kernel_name = 'hybrid_pool_fox_moe_block'

def rms_norm(x, g):
    xf = x.astype(jnp.float32)
    y = xf * lax.rsqrt(jnp.mean(xf * xf, axis=-1, keepdims=True) + RMS_EPS)
    return (y * g.astype(jnp.float32)).astype(x.dtype)

def pool_mixer(u, w_pool, pool_scale):
    B, S, _ = u.shape
    uf = u.astype(jnp.float32)
    cs = jnp.cumsum(uf, axis=1)
    t = jnp.arange(S)
    outs = []
    for gi, w in enumerate(POOL_WINDOWS):
        sl = slice(gi * POOL_GROUP, (gi + 1) * POOL_GROUP)
        c = cs[:, :, sl]
        lower = jnp.pad(c[:, :S - w], ((0, 0), (w, 0), (0, 0)))
        cnt = jnp.minimum(t + 1, w).astype(jnp.float32)
        outs.append((c - lower) / cnt[None, :, None] - uf[:, :, sl])
    p = jnp.stack(outs, axis=2).astype(u.dtype)
    y = jnp.einsum('bsgc,gcd->bsgd', p, w_pool).reshape(B, S, POOL_WIDTH)
    return y * pool_scale

def forgetting_attention(q, k, v, log_f):
    B, H, S, Dh = q.shape
    c = jnp.cumsum(log_f, axis=-1)
    kf = k.astype(jnp.float32)
    key_pos = jnp.arange(S)
    scale = HEAD_DIM ** -0.5

    def block(i):
        start = i * Q_BLOCK
        qb = lax.dynamic_slice_in_dim(q, start, Q_BLOCK, axis=2).astype(jnp.float32)
        cb = lax.dynamic_slice_in_dim(c, start, Q_BLOCK, axis=2)
        logits = jnp.einsum('bhqd,bhkd->bhqk', qb, kf) * scale + cb[..., :, None] - c[..., None, :]
        q_pos = start + jnp.arange(Q_BLOCK)
        mask = key_pos[None, :] <= q_pos[:, None]
        logits = jnp.where(mask, logits, -jnp.inf)
        p = jax.nn.softmax(logits, axis=-1)
        return jnp.einsum('bhqk,bhkd->bhqd', p.astype(v.dtype), v)

    out = lax.map(block, jnp.arange(S // Q_BLOCK))
    return jnp.moveaxis(out, 0, 2).reshape(B, H, S, Dh)

def clamped_swiglu(a):
    x_glu, x_lin = a[..., :D_EXPERT], a[..., D_EXPERT:]
    x_glu = jnp.minimum(x_glu, SWIGLU_LIMIT)
    x_lin = jnp.clip(x_lin, -SWIGLU_LIMIT, SWIGLU_LIMIT)
    return x_glu * jax.nn.sigmoid(SWIGLU_ALPHA * x_glu) * (x_lin + 1.0)

def moe_ffn(h, w_router, b_router, w_up, b_up, w_down, b_down):
    B, S, D = h.shape
    T = B * S
    hf = h.reshape(T, D)
    logits = (hf @ w_router).astype(jnp.float32) + b_router.astype(jnp.float32)
    top_vals, top_idx = lax.top_k(logits, TOP_K)
    gates = jax.nn.softmax(top_vals, axis=-1)
    n_assign = T * TOP_K
    flat_e = top_idx.reshape(-1).astype(jnp.int32)
    flat_tok = jnp.arange(n_assign, dtype=jnp.int32) // TOP_K
    order = jnp.argsort(flat_e)
    sorted_e = flat_e[order]
    sorted_tok = flat_tok[order]
    sorted_gate = gates.reshape(-1)[order]
    counts = jnp.bincount(flat_e, length=N_EXPERTS)
    starts = jnp.cumsum(counts) - counts
    padded = (counts + EXPERT_BLOCK - 1) // EXPERT_BLOCK * EXPERT_BLOCK
    pad_ends = jnp.cumsum(padded)
    pad_starts = pad_ends - padded
    dest = pad_starts[sorted_e] + (jnp.arange(n_assign, dtype=jnp.int32) - starts[sorted_e])
    n_rows = n_assign + N_EXPERTS * EXPERT_BLOCK
    n_blocks = n_rows // EXPERT_BLOCK
    row_tok = jnp.full((n_rows,), T, jnp.int32).at[dest].set(sorted_tok)
    row_gate = jnp.zeros((n_rows,), jnp.float32).at[dest].set(sorted_gate)
    block_e = jnp.minimum(
        jnp.searchsorted(pad_ends, jnp.arange(n_blocks) * EXPERT_BLOCK, side='right'),
        N_EXPERTS - 1)
    h_pad = jnp.concatenate([hf, jnp.zeros((1, D), hf.dtype)], axis=0)
    xs = h_pad[row_tok].reshape(n_blocks, EXPERT_BLOCK, D)

    def expert_block(args):
        xb, e = args
        a = xb @ w_up[e] + b_up[e]
        return clamped_swiglu(a) @ w_down[e] + b_down[e]

    ys = lax.map(expert_block, (xs, block_e)).reshape(n_rows, D)
    contrib = ys.astype(jnp.float32) * row_gate[:, None]
    out = jax.ops.segment_sum(contrib, row_tok, num_segments=T + 1)[:T]
    return out.reshape(B, S, D).astype(h.dtype)

def setup_inputs(seed: int = 0) -> dict:
    key = jax.random.key(seed)
    ks = jax.random.split(key, 16)
    f32 = jnp.float32
    L = DEPTH

    def nrm(k, shape, scale):
        return jax.random.normal(k, shape, f32) * scale

    return {
        'x': nrm(ks[0], (BATCH, SEQ, D_MODEL), 1.0),
        'g_mix': 1.0 + nrm(ks[1], (L, D_MODEL), 0.05),
        'w_in': nrm(ks[2], (L, D_MODEL, IN_WIDTH), D_MODEL ** -0.5),
        'b_forget': 2.0 + nrm(ks[3], (L, N_HEADS), 0.5),
        'w_pool': nrm(ks[4], (L, N_POOL_GROUPS, POOL_GROUP, POOL_GROUP), POOL_GROUP ** -0.5),
        'pool_scale': 1.0 + nrm(ks[5], (L, POOL_WIDTH), 0.1),
        'w_out': nrm(ks[6], (L, D_MODEL, D_MODEL), D_MODEL ** -0.5),
        'g_ffn': 1.0 + nrm(ks[7], (L, D_MODEL), 0.05),
        'w_router': nrm(ks[8], (L, D_MODEL, N_EXPERTS), D_MODEL ** -0.5),
        'b_router': nrm(ks[9], (L, N_EXPERTS), 0.01),
        'w_up': nrm(ks[10], (L, N_EXPERTS, D_MODEL, 2 * D_EXPERT), D_MODEL ** -0.5),
        'b_up': nrm(ks[11], (L, N_EXPERTS, 2 * D_EXPERT), 0.01),
        'w_down': nrm(ks[12], (L, N_EXPERTS, D_EXPERT, D_MODEL), D_EXPERT ** -0.5),
        'b_down': nrm(ks[13], (L, N_EXPERTS, D_MODEL), 0.01),
        'g_final': 1.0 + nrm(ks[14], (D_MODEL,), 0.05),
    }

def reference(x, g_mix, w_in, b_forget, w_pool, pool_scale, w_out, g_ffn,
              w_router, b_router, w_up, b_up, w_down, b_down, g_final):
    B, S, D = x.shape
    for l in range(DEPTH):
        h = rms_norm(x, g_mix[l])
        proj = h @ w_in[l]
        o = POOL_WIDTH
        u = proj[..., :o]
        q = proj[..., o:o + ATTN_WIDTH]
        k = proj[..., o + ATTN_WIDTH:o + 2 * ATTN_WIDTH]
        v = proj[..., o + 2 * ATTN_WIDTH:o + 3 * ATTN_WIDTH]
        f_logit = proj[..., o + 3 * ATTN_WIDTH:]
        to_heads = lambda t: t.reshape(B, S, N_HEADS, HEAD_DIM).transpose(0, 2, 1, 3)
        log_f = jax.nn.log_sigmoid(f_logit.astype(jnp.float32) + b_forget[l].astype(jnp.float32))
        log_f = log_f.transpose(0, 2, 1)
        y_pool = pool_mixer(u, w_pool[l], pool_scale[l])
        y_attn = forgetting_attention(to_heads(q), to_heads(k), to_heads(v), log_f)
        y_attn = y_attn.transpose(0, 2, 1, 3).reshape(B, S, ATTN_WIDTH)
        x = x + jnp.concatenate([y_pool, y_attn], axis=-1) @ w_out[l]
        h2 = rms_norm(x, g_ffn[l])
        x = x + moe_ffn(h2, w_router[l], b_router[l], w_up[l], b_up[l], w_down[l], b_down[l])
    return rms_norm(x, g_final)


_drawn_inputs = setup_inputs


def setup_inputs(seed=0):
    import zlib

    import numpy as np

    out = dict(_drawn_inputs(seed))
    spreads = {}
    factors = {'b_up': 8.0, 'b_down': 8.0}
    for name, (base, spread) in spreads.items():
        noise = np.random.default_rng([zlib.crc32(name.encode()), seed]).standard_normal(out[name].shape)
        drawn = base * np.exp(spread * noise) if base else spread * noise
        out[name] = __import__('jax').numpy.asarray(drawn.astype(out[name].dtype))
    for name, factor in factors.items():
        out[name] = (out[name] * factor).astype(out[name].dtype)
    return out
```

```python
from contextlib import ExitStack

import numpy as np
import concourse.bass as bass
from concourse import mybir

F32 = mybir.dt.float32
F32R = mybir.dt.float32r
BF16 = mybir.dt.bfloat16
I32 = mybir.dt.int32
U32 = mybir.dt.uint32
ALU = mybir.AluOpType
ACT = mybir.ActivationFunctionType
AX = mybir.AxisListType

P = 128
D = 1024
S = 1024
KT = D // P
NT = S // P
PW = 512
NG = 4
PAD = 16
AW = 512
HD = 64
NH = AW // HD
NE = 32
TOPK = 4
EPS = 1e-5
LIMIT = 7.0
ALPHA = 1.702
NEG = -1.0e30

CW = 512
HW_ = 256
RAW = 3
RING = 4
PRO_PIECES = 12
SLOTS = 192
MAX_ITEMS = 53
ITEMS = 56
NCH = 6
NPC = 2 * NCH
WIDTHS = (128, 160, SLOTS)
ROW = D + NE


class Map:

    def __init__(self, nc, at, end):
        self.nc, self.at, self.end = nc, at, end

    def take(self, name, shape, dt, at=None):
        size = 1
        for n in shape[1:]:
            size *= n
        size *= 2 if dt == BF16 else 4
        off = self.at if at is None else at
        if at is None:
            self.at += (size + 31) // 32 * 32
            assert self.at <= self.end, (name, self.at, self.end)
        return self.nc.alloc_sbuf_tensor_at(name, shape, dt, offset=off)


def build(nc, x, g_mix, w_in, b_forget, w_pool, pool_scale, w_out, g_ffn, w_router, b_router,
          w_up, b_up, w_down, b_down, g_final, ident_in, out, phases=9, dbg=None):
    ctx = ExitStack()
    with ctx:
        def sem(name):
            return ctx.enter_context(nc.semaphore(name))

        x_rows = x.rearrange("b s d -> (b s) d")
        out_rows = out.rearrange("b s d -> (b s) d")

        qk_d = nc.dram_tensor("qk_d", [4, AW, S], F32).ap()
        v_d = nc.dram_tensor("v_d", [S, NH, 2, HD], F32).ap()
        negc_d = nc.dram_tensor("negc_d", [2, NH, S], F32).ap()
        yp_d = nc.dram_tensor("yp_d", [PW, S], F32).ap()
        h2g_d = nc.dram_tensor("h2g_d", [S, ROW], F32).ap()
        acc_d = nc.dram_tensor("acc_d", [S, D], F32).ap()

        keep = Map(nc, (nc.sbuf_base + 31) // 32 * 32, nc.sbuf_usable_end)
        raw = [keep.take(f"raw{i}", [P, KT, CW], F32) for i in range(RAW)]
        ident = keep.take("ident", [P, P], F32)
        identb = keep.take("identb", [P, P], BF16)
        one = keep.take("one", [P, 1], F32)
        epsb = keep.take("eps", [P, 1], F32)
        top = keep.at

        def ring(m):
            wh = [m.take(f"wh{i}_{m.tag}", [P, KT, HW_], F32R) for i in range(RING)]
            wl = [m.take(f"wl{i}_{m.tag}", [P, KT, HW_], F32R) for i in range(RING)]
            return wh, wl

        def phase(tag):
            m = Map(nc, top, nc.sbuf_usable_end)
            m.tag = tag
            return m

        ps = ctx.enter_context(nc.psum_tensor("ps", [P, 8 * 512], F32))
        psum = [ps[:, i * 512:(i + 1) * 512] for i in range(8)]
        psum2 = [ps[:, i * 1024:(i + 1) * 1024] for i in range(4)]

        s_raw = [sem(f"raw_landed{i}") for i in range(RAW)]
        s_hi = sem("piece_hi")
        s_lo = sem("piece_lo")
        s_pd = sem("piece_used")

        def cols(w, c0, n=CW):
            return w[:, c0:c0 + n].rearrange("(k p) n -> p k n", p=P)

        def item_chunk(e, c):
            w, c0 = (w_up, (0, D, CW, D + CW)[c]) if c < 4 else (w_down, (c - 4) * CW)
            return w[0, bass.ds(e, 1), :, c0:c0 + CW].rearrange("e (k p) n -> p (e k) n", p=P)

        w_in0 = w_in[0]
        w_out0 = w_out[0]
        pro_chunks = [cols(w_in0, PW + 2 * AW), cols(w_in0, PW), cols(w_in0, PW + AW), cols(w_in0, 0),
                      cols(w_out0, 0), cols(w_out0, CW)]

        def load_chunk(sp, n, src):
            if n >= RAW:
                sp.wait_ge(s_lo, 2 * (n - RAW) + 2)
            sp.dma_start(raw[n % RAW][:], src).then_inc(s_raw[n % RAW], 16)

        def raw_piece(p):
            return raw[(p // 2) % RAW][:, :, (p % 2) * HW_:(p % 2 + 1) * HW_]

        def split_hi(act, wh, p):
            act.wait_ge(s_raw[(p // 2) % RAW], 16 * (p // 2 // RAW + 1))
            act.activation(wh[p % RING][:], raw_piece(p), ACT.Copy).then_inc(s_hi, 1)

        def split_lo(dve, wh, wl, p):
            dve.wait_ge(s_hi, p + 1)
            dve.tensor_tensor(wl[p % RING][:], raw_piece(p), wh[p % RING][:].bitcast(F32),
                              ALU.subtract).then_inc(s_lo, 1)

        m = phase("proj")
        wh, wl = ring(m)
        hh = m.take("h_hi", [P, KT, S], F32R)
        hl = m.take("h_lo", [P, KT, S], F32R)
        xa = m.at
        xt = [m.take(f"xt{i}", [P, D], F32) for i in range(2)]
        xn = m.take("xn", [P, D], F32)
        grow = m.take("g_mix_row", [P, D], F32)
        m.at = xa
        nl = m.take("neg_logf", [NH, S], F32, at=xa)
        negc = m.take("neg_c", [NH, S], F32, at=xa + 4096)
        nhi = m.take("neg_c_hi", [NH, S], F32R, at=xa + 8192)
        nlo = m.take("neg_c_lo", [NH, S], F32R, at=xa + 12288)
        ub = [m.take(f"u{i}", [P, PAD + S], F32) for i in range(4)]
        stage_at = m.at
        stage = [[m.take(f"st{i}{j}", [P, 512], F32R) for j in "hl"] for i in range(2)]
        wp = m.take("w_pool_sb", [P, NG, P], F32)
        wf = m.take("w_f", [P, KT, NH], F32)
        wfh = m.take("w_f_hi", [P, KT, NH], F32R)
        wfl = m.take("w_f_lo", [P, KT, NH], F32R)
        psc = m.take("pool_scale_col", [P, NG], F32)
        bfr = m.take("b_forget_row", [P, NH], F32)
        fz = [m.take(f"fz{i}", [P, NT, NH], F32) for i in range(4)]
        rc = m.take("rcount", [P, PAD], F32)
        sqj = m.take("square_dump", [P, D], BF16)
        ssq = m.take("ssq", [P, NT], F32)
        rst = m.take("rstd", [P, 2 * NT], F32)

        NV, NQK, NU = 16, 16, 8
        GRP = NV + NQK + NU
        SPLIT_AT = {NT: 4, NV: 5, NV + 4: 6, NV + 8: 7}
        s_x = [sem(f"x_landed{i}") for i in range(2)]
        s_c = sem("proj_consts")
        s_c2 = sem("pool_consts")
        s_sq = sem("x_squares")
        s_eps = sem("eps_set")
        s_rs = sem("x_rstd")
        s_xn = sem("x_normed")
        s_tr = sem("h_transposed")
        s_hh = sem("h_hi_done")
        s_hl = sem("h_lo_done")
        s_g = sem("proj_group")
        s_gh = sem("proj_group_hi")
        s_gl = sem("proj_group_lo")
        s_st = [sem(f"proj_stored{i}") for i in range(2)]
        s_wf = sem("w_f_split")
        s_f = sem("forget_logits")
        s_fv = sem("forget_dve")
        s_fa = sem("forget_act")
        s_ft = sem("forget_transposed")
        s_nc = sem("neg_c_stored")
        s_rc = sem("rcount_set")
        s_uv = sem("pool_dve")
        s_pm = sem("pool_product")
        s_pe = sem("pool_evacuated")
        s_ps = sem("pool_stored")
        s_id = sem("identity_bf16")

        with nc.Block() as block:
            @block.sync
            def _(sp):
                sp.dma_start(ident[:], ident_in).then_inc(s_c, 16)
                sp.dma_start(grow[:], g_mix.to_broadcast([P, D])).then_inc(s_c, 16)
                for i in range(NT):
                    if i >= 2:
                        sp.wait_ge(s_xn, i - 1)
                    sp.dma_start(xt[i % 2][:], x_rows[i * P:(i + 1) * P, :]).then_inc(s_x[i % 2], 16)
                    if i == 0:
                        load_chunk(sp, 0, pro_chunks[0])
                        sp.dma_start(wf[:], cols(w_in0, PW + 3 * AW, NH)).then_inc(s_c, 16)
                        sp.dma_start(bfr[:], b_forget.to_broadcast([P, NH])).then_inc(s_c, 16)
                    if i in (1, 3):
                        load_chunk(sp, (i + 1) // 2, pro_chunks[(i + 1) // 2])
                    if i == 4:
                        sp.dma_start(psc[:], pool_scale[0].rearrange("(g p) -> p g", p=P),
                                     allow_slow_non_contiguous=True).then_inc(s_c2, 16)
                        sp.dma_start(wp[:], w_pool[0].rearrange("g c d -> c g d")).then_inc(s_c2, 16)
                for n in range(3, 6):
                    load_chunk(sp, n, pro_chunks[n])

            @block.gpsimd
            def _(pool):
                for t in range(PAD):
                    pool.memset(rc[:, t:t + 1], 1.0 / (t + 1)).then_inc(s_rc, 1)
                pool.memset(epsb[:], EPS).then_inc(s_eps, 1)
                pool.memset(one[:], 1.0).then_inc(s_eps, 1)

                for n in range(NV + NQK):
                    pool.wait_ge(s_gl, n + 1)
                    for part in range(2):
                        if n < NV:
                            pc, i = divmod(n, NT)
                            dst = v_d[i * P:(i + 1) * P, 4 * pc:4 * pc + 4, part, :]
                            src = stage[n % 2][part][:, 0:HW_].rearrange("p (h d) -> p h d", h=4)
                        else:
                            ft, half = divmod(n - NV, 2)
                            dst = qk_d[2 * (ft // 4) + part, (ft % 4) * P:(ft % 4 + 1) * P, half * 512:half * 512 + 512]
                            src = stage[n % 2][part][:]
                        pool.dma_start(dst, src.bitcast(F32)).then_inc(s_st[n % 2], 16)
                pool.wait_ge(s_st[0], 16 * (NV + NQK))
                pool.wait_ge(s_st[1], 16 * (NV + NQK))
                for g in range(NG):
                    pool.wait_ge(s_pe, 2 * g + 2)
                    pool.dma_start(yp_d[g * P:(g + 1) * P, :], ub[3][:, 0:S]).then_inc(s_ps, 16)
                pool.wait_ge(s_ps, 16 * NG)

            def evac_hi(act, n):
                act.wait_ge(s_g, n + 1)
                if n >= 2:
                    act.wait_ge(s_st[n % 2], 32 * (n // 2))
                w = HW_ if n < NV else 512
                q_half = NV <= n < NV + NQK // 2
                act.activation(stage[n % 2][0][:, 0:w], psum[n % 4][:, 0:w], ACT.Copy,
                               scale=HD ** -0.5 if q_half else 1.0).then_inc(s_gh, 1)

            def evac_lo(dve, n):
                dve.wait_ge(s_gh, n + 1)
                w = HW_ if n < NV else 512
                q_half = NV <= n < NV + NQK // 2
                dve.scalar_tensor_tensor(out=stage[n % 2][1][:, 0:w], in0=psum[n % 4][:, 0:w],
                                         scalar=HD ** -0.5 if q_half else 1.0,
                                         in1=stage[n % 2][0][:, 0:w].bitcast(F32),
                                         op0=ALU.mult, op1=ALU.subtract).then_inc(s_gl, 1)

            def forget_act(act):
                act.wait_ge(s_fv, 2)
                act.activation(fz[2][:], fz[1][:], ACT.Exp, scale=-1.0).then_inc(s_fa, 1)
                act.wait_ge(s_fa, 1)
                act.activation(fz[3][:], fz[2][:], ACT.Ln, bias=one[:]).then_inc(s_fa, 1)
                for b in range(2):
                    act.wait_ge(s_ft, b + 1)
                    act.activation(nl[:, b * 512:(b + 1) * 512], psum[4 + b][0:NH, :], ACT.Copy,
                                   scale=-1.0).then_inc(s_fa, 1)
                act.wait_ge(s_fv, 4)
                act.activation(nhi[:], negc[:], ACT.Copy).then_inc(s_fa, 1)
                act.wait_ge(s_fv, 5)
                for part, t in enumerate((nhi, nlo)):
                    act.dma_start(negc_d[part], t[:].bitcast(F32)).then_inc(s_nc, 16)

            POOL_DONE = []
            done = 3   
            for g in range(NG):
                done += (g + 1) + 3
                POOL_DONE.append(done)

            def pool_out(act, g):
                if g == 0:
                    act.wait_ge(s_c2, 32)
                for half in range(2):
                    act.wait_ge(s_pm, 2 * g + half + 1)
                    if g >= 1 and half == 0:
                        act.wait_ge(s_ps, 16 * g)
                    act.activation(ub[3][:, half * 512:half * 512 + 512], psum[6 + half][:], ACT.Copy,
                                   scale=psc[:, g:g + 1]).then_inc(s_pe, 1)

            def pool_product(pe, g):
                pe.wait_ge(s_uv, POOL_DONE[g])
                if g == 0:
                    pe.wait_ge(s_c2, 32)
                p = ub[1 + (g + 1) % 2]
                for half in range(2):
                    if g >= 1:
                        pe.wait_ge(s_pe, 2 * (g - 1) + half + 1)
                    pe.matmul(psum[6 + half][:], wp[:, g, :], p[:, PAD + half * 512:PAD + half * 512 + 512],
                              start=True, stop=True).then_inc(s_pm, 1)

            @block.scalar
            def _(act):
                act.wait_ge(s_c, 64)
                act.activation(identb[:], ident[:], ACT.Copy).then_inc(s_id, 1)
                act.activation(wfh[:], wf[:], ACT.Copy).then_inc(s_wf, 1)
                act.wait_ge(s_eps, 2)

                def squares(i):
                    act.wait_ge(s_x[i % 2], 16 * (i // 2 + 1))
                    if i >= 1:
                        act.wait_ge(s_sq, 2 * i)
                    act.activation(sqj[:], xt[i % 2][:], ACT.Square, accum_out=ssq[:, i:i + 1]).then_inc(s_sq, 1)
                    act.wait_ge(s_sq, 2 * i + 1)
                    act.activation(rst[:, i:i + 1], ssq[:, i:i + 1], ACT.Sqrt, bias=epsb[:],
                                   scale=1.0 / D).then_inc(s_sq, 1)

                squares(0)
                for i in range(NT):
                    if i + 1 < NT:
                        squares(i + 1)
                    if i < RING:
                        split_hi(act, wh, i)
                    for b in range(2):
                        act.wait_ge(s_tr, 2 * i + b + 1)
                        act.activation(hh[:, 4 * b:4 * b + 4, i * P:(i + 1) * P],
                                       psum[4 + b][:].rearrange("p (k t) -> p k t", k=4), ACT.Copy).then_inc(s_hh, 1)
                    if i >= 1:
                        evac_hi(act, i - 1)
                evac_hi(act, NT - 1)
                for n in range(NT, GRP):
                    if n in SPLIT_AT:
                        act.wait_ge(s_g, n)
                        split_hi(act, wh, SPLIT_AT[n])
                    if n == NV:
                        forget_act(act)
                    if n < NV + NQK:
                        evac_hi(act, n)
                    else:
                        g, half = divmod(n - NV - NQK, 2)
                        if g >= 1 and half == 0:
                            act.wait_ge(s_uv, POOL_DONE[g - 1])
                        if n == NV + NQK:
                            act.wait_ge(s_nc, 32)
                        act.wait_ge(s_g, n + 1)
                        act.activation(ub[0][:, PAD + half * 512:PAD + half * 512 + 512], psum[n % 4][:],
                                       ACT.Copy).then_inc(s_gh, 1)
                        if half == 1 and g >= 1:
                            pool_out(act, g - 1)
                pool_out(act, NG - 1)

            @block.vector
            def _(dve):
                dve.wait_ge(s_wf, 1)
                dve.tensor_tensor(wfl[:], wf[:], wfh[:].bitcast(F32), ALU.subtract).then_inc(s_wf, 1)

                def h_lo(i):
                    for b in range(2):
                        dve.wait_ge(s_hh, 2 * i + b + 1)
                        dve.tensor_tensor(hl[:, 4 * b:4 * b + 4, i * P:(i + 1) * P],
                                          psum[4 + b][:].rearrange("p (k t) -> p k t", k=4),
                                          hh[:, 4 * b:4 * b + 4, i * P:(i + 1) * P].bitcast(F32),
                                          ALU.subtract).then_inc(s_hl, 1)

                for i in range(NT):
                    dve.wait_ge(s_sq, 2 * i + 2)
                    dve.reciprocal(rst[:, NT + i:NT + i + 1], rst[:, i:i + 1]).then_inc(s_rs, 1)
                    dve.wait_ge(s_rs, i + 1)
                    dve.scalar_tensor_tensor(out=xn[:], in0=xt[i % 2][:], scalar=rst[:, NT + i:NT + i + 1],
                                             in1=grow[:], op0=ALU.mult, op1=ALU.mult).then_inc(s_xn, 1)
                    if i < RING:
                        split_lo(dve, wh, wl, i)
                    h_lo(i)
                    if i >= 1:
                        evac_lo(dve, i - 1)
                evac_lo(dve, NT - 1)

                def forget_dve():
                    dve.wait_ge(s_f, 1)
                    dve.tensor_tensor(fz[0][:], psum[6][:, 0:NT * NH].rearrange("p (i h) -> p i h", i=NT),
                                      bfr[:].unsqueeze(1).to_broadcast([P, NT, NH]), ALU.add).then_inc(s_fv, 1)
                    dve.wait_ge(s_fv, 1)
                    dve.scalar_tensor_tensor(out=fz[1][:], in0=fz[0][:], scalar=-1.0, in1=fz[0][:],
                                             op0=ALU.mult, op1=ALU.max).then_inc(s_fv, 1)
                    dve.wait_ge(s_fa, 2)
                    dve.scalar_tensor_tensor(out=fz[2][:], in0=fz[0][:], scalar=0.0, in1=fz[3][:],
                                             op0=ALU.min, op1=ALU.subtract).then_inc(s_fv, 1)
                    dve.wait_ge(s_fa, 4)
                    dve.tensor_tensor_scan(negc[:], nl[:], nl[:], 0.0, ALU.add, ALU.max).then_inc(s_fv, 1)
                    dve.wait_ge(s_fa, 5)
                    dve.tensor_tensor(nlo[:], negc[:], nhi[:].bitcast(F32), ALU.subtract).then_inc(s_fv, 1)

                for n in range(NT, NV + NQK):
                    if n in SPLIT_AT:
                        split_lo(dve, wh, wl, SPLIT_AT[n])
                    if n == NV:
                        forget_dve()
                    evac_lo(dve, n)
                dve.wait_ge(s_rc, PAD)
                dve.wait_ge(s_nc, 32)
                for b in range(3):
                    dve.memset(ub[b][:, 0:PAD], 0.0).then_inc(s_uv, 1)
                cnt = 3
                for g in range(NG):
                    dve.wait_ge(s_gh, NV + NQK + 2 * g + 2)
                    if g == 0:
                        dve.wait_ge(s_uv, 3)
                    src, w = ub[0], 1
                    for lev in range(g + 1):
                        dst = ub[1 + lev % 2]
                        if lev >= 1:
                            dve.wait_ge(s_uv, cnt)
                        elif g >= 1:
                            dve.wait_ge(s_pm, 2 * g)
                        dve.tensor_tensor(dst[:, PAD:], src[:, PAD:], src[:, PAD - w:PAD + S - w],
                                          ALU.add).then_inc(s_uv, 1)
                        cnt += 1
                        src, w = dst, 2 * w
                    other = ub[1 + (g + 1) % 2]
                    dve.wait_ge(s_uv, cnt)
                    dve.scalar_tensor_tensor(out=other[:, PAD:], in0=src[:, PAD:], scalar=1.0 / w,
                                             in1=ub[0][:, PAD:], op0=ALU.mult, op1=ALU.subtract).then_inc(s_uv, 1)
                    cnt += 1
                    dve.wait_ge(s_uv, cnt)
                    dve.tensor_tensor(src[:, PAD:PAD + w - 1], src[:, PAD:PAD + w - 1], rc[:, 0:w - 1], ALU.mult).then_inc(s_uv, 1)
                    cnt += 1
                    dve.wait_ge(s_uv, cnt)
                    dve.tensor_tensor(other[:, PAD:PAD + w - 1], src[:, PAD:PAD + w - 1],
                                      ub[0][:, PAD:PAD + w - 1], ALU.subtract).then_inc(s_uv, 1)
                    cnt += 1

            @block.tensor
            def _(pe):
                pe.wait_ge(s_c, 64)

                def group_wait(n):
                    if n >= 4:
                        if n - 4 < NV + NQK:
                            pe.wait_ge(s_gl, n - 3)
                        else:
                            pe.wait_ge(s_gh, n - 3)

                def v_group(n):
                    pc, i = divmod(n, NT)
                    group_wait(n)
                    pe.wait_ge(s_hl, 2 * i + 2)
                    if i == 0 or pc == 0:
                        pe.wait_ge(s_lo, pc + 1)
                    o = psum[n % 4][:, 0:HW_]
                    for k in range(KT):
                        tok = slice(i * P, (i + 1) * P)
                        pe.matmul(o, hh[:, k, tok], wh[pc][:, k, :], start=(k == 0), stop=False)
                        pe.matmul(o, hh[:, k, tok], wl[pc][:, k, :], start=False, stop=False)
                        last = pe.matmul(o, hl[:, k, tok], wh[pc][:, k, :], start=False, stop=(k == KT - 1))
                    last.then_inc(s_g, 1)
                    return last

                for i in range(NT):
                    pe.wait_ge(s_xn, i + 1)
                    for b in range(2):
                        if i >= 1:
                            pe.wait_ge(s_hl, 2 * (i - 1) + b + 1)
                        for j in range(4):
                            k = 4 * b + j
                            last = pe.transpose(psum[4 + b][:, j * P:(j + 1) * P], xn[:, k * P:(k + 1) * P], ident[:])
                        last.then_inc(s_tr, 1)
                    if i >= 1:
                        v_group(i - 1)
                v_group(NT - 1)
                for n in range(NT, NV):
                    v_group(n)
                pe.wait_ge(s_wf, 2)
                for i in range(NT):
                    for k in range(KT):
                        tok = slice(i * P, (i + 1) * P)
                        o = psum[6][:, i * NH:(i + 1) * NH]
                        pe.matmul(o, hh[:, k, tok], wfh[:, k, :], start=(k == 0), stop=False)
                        pe.matmul(o, hh[:, k, tok], wfl[:, k, :], start=False, stop=False)
                        last = pe.matmul(o, hl[:, k, tok], wfh[:, k, :], start=False, stop=(k == KT - 1))
                last.then_inc(s_f, 1)
                n = NV
                for p in range(2, 8):
                    for t in range(2):
                        for half in range(2):
                            group_wait(n)
                            pe.wait_ge(s_lo, p + 1)
                            o = psum[n % 4][:]
                            f = slice(t * P, (t + 1) * P)
                            tok = slice(half * 512, (half + 1) * 512)
                            sl = p % RING
                            for k in range(KT):
                                pe.matmul(o, wh[sl][:, k, f], hh[:, k, tok], start=(k == 0), stop=False)
                                pe.matmul(o, wh[sl][:, k, f], hl[:, k, tok], start=False, stop=False)
                                last = pe.matmul(o, wl[sl][:, k, f], hh[:, k, tok], start=False, stop=(k == KT - 1))
                            last.then_inc(s_g, 1)
                            n += 1
                            if n == NV + 2:
                                pe.wait_ge(s_fv, 3)
                                for i in range(NT):
                                    tr = pe.transpose(psum[4 + i // 4][0:NH, (i % 4) * P:(i % 4 + 1) * P],
                                                      fz[2][:, i, :], ident[:])
                                    if i % 4 == 3:
                                        tr.then_inc(s_ft, 1)
                            if n > NV + NQK and (n - NV - NQK) % 2 == 0 and n - NV - NQK >= 4:
                                pool_product(pe, (n - NV - NQK) // 2 - 2)
                pool_product(pe, NG - 1)


        if phases < 2:
            return

        m = phase("attn")
        m.at = nc.sbuf_usable_end // 32 * 32 - 4 * S * 4
        ya = m.take("y_attn", [P, 4, S], F32)
        m.at = top
        m.end = nc.sbuf_usable_end // 32 * 32 - 4 * S * 4
        QA = [m.take(f"qa{i}", [P, S], F32R) for i in range(2)]
        KA = [m.take(f"ka{i}", [P, S], F32R) for i in range(2)]
        QB = [m.take(f"qb{i}", [P, S], F32R) for i in range(2)]
        KB = [m.take(f"kb{i}", [P, S], F32R) for i in range(2)]
        VV = [m.take(f"vv{i}", [P, NT, P], F32R) for i in range(2)]
        pr = [m.take(f"prob{i}", [P, S], F32) for i in range(2)]
        pth = [m.take(f"pt_hi{i}", [P, NT, 2 * P], F32R) for i in range(2)]
        ptl = [m.take(f"pt_lo{i}", [P, NT, 2 * P], F32R) for i in range(2)]
        otmp = [m.take(f"o_tmp{i}", [HD, 2 * P], F32) for i in range(2)]
        nmx = m.take("neg_max", [P, 16], F32)
        rsm = m.take("row_sum", [P, 16], F32)
        rrs = m.take("row_sum_inv", [P, 16], F32)
        maskb = m.take("mask", [P, P], BF16)
        onesf = m.take("ones_f", [P, S], F32)

        QT = 2 * NT
        NB = [1] * 4 + [2] * 4
        TB = 2 * sum(NB)
        first_bank = [sum(NB[:i]) for i in range(NT)]
        s_ld = [sem(f"head_landed{i}") for i in range(2)]
        s_on = sem("attn_consts")
        s_S = sem("logits")
        s_nm = sem("neg_max_done")
        s_P = sem("exp_done")
        s_rr = sem("row_sum_inv_done")
        s_Pn = sem("prob_normed")
        s_T = sem("prob_transposed")
        s_Th = sem("pt_hi_done")
        s_Tl = sem("pt_lo_done")
        s_O = sem("attn_product")
        s_Oa = sem("o_tmp_done")
        s_Oy = sem("y_attn_done")

        with nc.Block() as block:
            @block.sync
            def _(sp):
                def load_head(h, s):
                    q = bass.ds(h * HD, HD)
                    lo_half = slice(HD, 2 * HD)
                    for dst, src in ((QA[s][0:HD], qk_d[0, q]), (QA[s][lo_half], qk_d[1, q]),
                                     (KA[s][0:HD], qk_d[2, q]), (KA[s][lo_half], qk_d[2, q]),
                                     (QB[s][0:HD], qk_d[0, q]), (KB[s][0:HD], qk_d[3, q]),
                                     (KB[s][HD:HD + 2], negc_d[:, bass.ds(h, 1), :].rearrange("a h t -> (a h) t"))):
                        sp.dma_start(dst.bitcast(F32), src).then_inc(s_ld[s], 16)
                    sp.dma_start(VV[s][:].bitcast(F32),
                                 v_d[:, bass.ds(h, 1), :, :].rearrange("(k p) h a d -> p k (h a d)", p=P)
                                 ).then_inc(s_ld[s], 16)

                load_head(0, 0)
                load_head(1, 1)
                with sp.Fori(0, NH // 2 - 1) as j:
                    for s in range(2):
                        sp.wait_ge(s_O, 8 * j + 2 + 4 * (s + 1))
                        load_head(2 * j + 2 + s, s)

            @block.gpsimd
            def _(pool):
                pool.memset(onesf[:], 1.0).then_inc(s_on, 1)
                pool.memset(maskb[:], 0.0).then_inc(s_on, 1)
                pool.wait_ge(s_on, 2)
                pool.affine_select(out=maskb[:], in_=maskb[:], pattern=[[-1, P]], compare_op=ALU.is_ge,
                                   fill=NEG, base=0, channel_multiplier=1).then_inc(s_on, 1)
                with pool.Fori(0, NH // 2) as j:
                    for n in range(QT):
                        qi = n % NT
                        pool.wait_ge(s_rr, QT * j + n + 1)
                        w = (qi + 1) * P
                        pool.tensor_tensor(pr[n % 2][:, 0:w], pr[n % 2][:, 0:w], rrs[:, n:n + 1].to_broadcast([P, w]),
                                           ALU.mult).then_inc(s_Pn, 1)

            @block.scalar
            def _(act):
                act.sem_inc(s_P, 2)
                act.wait_ge(s_on, 3)
                for s in range(2):
                    act.activation(QB[s][HD:P], onesf[HD:P], ACT.Copy).then_inc(s_on, 1)
                with act.Fori(0, NH // 2) as j:
                    def exp(n):
                        w = (n % NT + 1) * P
                        act.wait_ge(s_nm, QT * j + n + 1)
                        act.wait_ge(s_T, TB * j + 3 + (first_bank[(n - 2) % NT] + NB[(n - 2) % NT]
                                                       + (TB // 2) * ((n - 2) // NT)))
                        src = psum2[n % 2][:, 0:w]
                        act.activation(pr[n % 2][:, 0:w], src, ACT.Exp, bias=nmx[:, n:n + 1],
                                       accum_out=rsm[:, n:n + 1]).then_inc(s_P, 1)

                    def pt_hi(n):
                        h2, qi = divmod(n, NT)
                        g = n // 2
                        for b in range(NB[qi]):
                            tb = (TB // 2) * h2 + first_bank[qi] + b
                            blocks = min(4, qi + 1 - 4 * b)
                            act.wait_ge(s_T, TB * j + 3 + tb + 1)
                            if b == 0 and n % 2 == 0:
                                act.wait_ge(s_O, 8 * j + g + 1)
                            act.activation(pth[g % 2][:, 4 * b:4 * b + blocks, (n % 2) * P:(n % 2 + 1) * P],
                                           psum[4 + tb % 2][:, 0:blocks * P].rearrange("p (k t) -> p k t", t=P),
                                           ACT.Copy).then_inc(s_Th, 1)

                    def o_tmp(g):
                        act.wait_ge(s_O, 8 * j + 2 + g + 1)
                        act.activation(otmp[g % 2][:], psum[6 + g % 2][HD:P, 0:2 * P], ACT.Copy).then_inc(s_Oa, 1)

                    exp(0)
                    for n in range(QT):
                        if n + 1 < QT:
                            exp(n + 1)
                        pt_hi(n)
                        if n % 2 == 0 and n >= 2:
                            o_tmp(n // 2 - 1)
                    o_tmp(QT // 2 - 1)

            @block.vector
            def _(dve):
                dve.sem_inc(s_Tl, 2)
                dve.sem_inc(s_Oy, 2)
                with dve.Fori(0, NH // 2) as j:
                    def neg_max(n):
                        w = (n % NT + 1) * P
                        dve.wait_ge(s_S, QT * j + n + 1)
                        dve.tensor_reduce(nmx[:, n:n + 1], psum2[n % 2][:, 0:w], AX.X, ALU.max,
                                          negate=True).then_inc(s_nm, 1)

                    def inv(n):
                        dve.wait_ge(s_P, QT * j + n + 3)
                        dve.reciprocal(rrs[:, n:n + 1], rsm[:, n:n + 1]).then_inc(s_rr, 1)

                    def pt_lo(n):
                        h2, qi = divmod(n, NT)
                        g = n // 2
                        for b in range(NB[qi]):
                            tb = (TB // 2) * h2 + first_bank[qi] + b
                            blocks = min(4, qi + 1 - 4 * b)
                            dve.wait_ge(s_Th, TB * j + tb + 1)
                            sl = (slice(None), slice(4 * b, 4 * b + blocks), slice((n % 2) * P, (n % 2 + 1) * P))
                            dve.tensor_tensor(ptl[g % 2][sl],
                                              psum[4 + tb % 2][:, 0:blocks * P].rearrange("p (k t) -> p k t", t=P),
                                              pth[g % 2][sl].bitcast(F32), ALU.subtract).then_inc(s_Tl, 1)

                    def y_out(g):
                        dve.wait_ge(s_Oa, 8 * j + g + 1)
                        hh_ = g // 4
                        dve.tensor_tensor(ya[HD * hh_:HD * hh_ + HD, bass.ds(j, 1), (g % 4) * 2 * P:(g % 4 + 1) * 2 * P],
                                          psum[6 + g % 2][0:HD, 0:2 * P].unsqueeze(1), otmp[g % 2][:].unsqueeze(1),
                                          ALU.add).then_inc(s_Oy, 1)

                    neg_max(0)
                    inv(0)
                    for n in range(QT):
                        if n + 1 < QT:
                            neg_max(n + 1)
                            inv(n + 1)
                        pt_lo(n)
                        if n % 2 == 0 and n >= 2:
                            y_out(n // 2 - 1)
                    y_out(QT // 2 - 1)

            @block.tensor
            def _(pe):
                pe.sem_inc(s_T, 3)
                pe.sem_inc(s_O, 2)
                pe.wait_ge(s_on, 5)
                with pe.Fori(0, NH // 2) as j:
                    def logits(n):
                        h2, qi = divmod(n, NT)
                        if qi == 0:
                            pe.wait_ge(s_ld[h2], 128 * j + 128)
                        pe.wait_ge(s_P, QT * j + n + 1)
                        q = slice(qi * P, (qi + 1) * P)
                        w = (qi + 1) * P
                        for c0 in range(0, w, 512):
                            c1 = min(c0 + 512, w)
                            o = psum2[n % 2][:, c0:c1]
                            diag = c1 == w
                            pe.matmul(o, QA[h2][:, q], KA[h2][:, c0:c1], start=True, stop=False)
                            last = pe.matmul(o, QB[h2][0:HD + 2, q], KB[h2][0:HD + 2, c0:c1], start=False, stop=not diag)
                            if diag:
                                last = pe.matmul(psum2[n % 2][:, w - P:w], identb[:], maskb[:], start=False, stop=True)
                        last.then_inc(s_S, 1)

                    def transposes(n):
                        h2, qi = divmod(n, NT)
                        pe.wait_ge(s_Pn, QT * j + n + 1)
                        for b in range(NB[qi]):
                            tb = (TB // 2) * h2 + first_bank[qi] + b
                            pe.wait_ge(s_Tl, TB * j + tb + 1)
                            for k in range(4 * b, min(4 * b + 4, qi + 1)):
                                last = pe.transpose(psum[4 + tb % 2][:, (k - 4 * b) * P:(k - 4 * b + 1) * P],
                                                    pr[n % 2][:, k * P:(k + 1) * P], ident[:])
                            last.then_inc(s_T, 1)

                    def product(g):
                        h2, gq = divmod(g, 4)
                        tb_end = (TB // 2) * h2 + first_bank[2 * gq + 1] + NB[2 * gq + 1]
                        pe.wait_ge(s_Tl, TB * j + 2 + tb_end)
                        pe.wait_ge(s_Oy, 8 * j + g + 1)
                        last_k = 2 * gq + 1
                        for k in range(last_k + 1):
                            c = P if k == last_k else 0
                            for part in (pth, ptl):
                                last = pe.matmul(psum[6 + g % 2][:, c:2 * P], VV[h2][:, k, :], part[g % 2][:, k, c:2 * P],
                                                 start=(k == 0 and part is pth), stop=(k == last_k and part is ptl))
                        last.then_inc(s_O, 1)

                    logits(0)
                    for n in range(QT):
                        if n + 1 < QT:
                            logits(n + 1)
                        transposes(n)
                        if n % 2 == 0 and n >= 2:
                            product(n // 2 - 1)
                    product(QT // 2 - 1)

        if phases < 3:
            return

        m = phase("mix")
        m.end = nc.sbuf_usable_end // 32 * 32 - 4 * S * 4
        posm_at = m.at
        msk = m.take("chosen", [P, NT, NE], BF16)
        wh, wl = ring(m)
        ypool = m.take("y_pool", [P, 4, S], F32)
        yh = [m.take(f"y_hi{i}", [P, KT, P], F32R) for i in range(2)]
        yl = m.take("y_lo", [P, KT, P], F32R)
        xr = m.take("x_res", [P, D], F32)
        x2 = [m.take(f"x2_{i}", [P, D], F32) for i in range(2)]
        h2r = [m.take(f"h2_row{i}", [P, ROW], F32) for i in range(2)]
        h2t = m.take("h2_t", [P, KT, P], F32)
        gfr = m.take("g_ffn_row", [P, D], F32)
        wr = m.take("w_router_sb", [P, KT, NE], F32)
        brr = m.take("b_router_row", [P, NE], F32)
        bdn = m.take("b_down_sb", [NE, D], F32)
        lg = m.take("router_logits", [P, NE], F32)
        top8 = m.take("top8", [P, 8], F32)
        ix8 = m.take("index8", [P, 8], U32)
        ixf = m.take("index_f", [P, TOPK], F32)
        ex = m.take("gate_exp", [P, TOPK], F32)
        tiny = m.take("tiny", [P, 8], F32)
        gat = m.take("gates", [P, TOPK], F32)
        ohe = m.take("one_hot", [P, TOPK, NE], F32)
        ohg = m.take("one_hot_gate", [P, TOPK, NE], F32)
        gtt = m.take("gates_t", [NE, P], F32)
        ioe = m.take("iota_e", [P, NE], F32)

        s_mc = sem("mix_consts")
        s_io = sem("iota_e_set")
        s_xr = sem("x_res_landed")
        s_yh = sem("y_hi_done")
        s_yl = sem("y_lo_done")
        s_og = sem("out_proj_done")
        s_x2 = sem("x2_done")
        s_ra = sem("router_act")
        s_rv = sem("router_dve")
        s_h2 = sem("h2_done")
        s_tt = sem("h2_transposed")
        s_te = sem("h2_t_done")
        s_rl = sem("router_product")
        s_gt = sem("gates_transposed")
        s_ge = sem("gates_t_done")
        s_bd = sem("bias_product")
        s_ac = sem("acc_done")
        s_hs = [sem(f"h2_stored{i}") for i in range(2)]
        s_as = [sem(f"acc_stored{i}") for i in range(2)]
        RV = 14

        with nc.Block() as block:
            @block.sync
            def _(sp):
                sp.dma_start(ypool[:], yp_d.rearrange("(g p) t -> p g t", p=P)).then_inc(s_mc, 16)
                sp.dma_start(gfr[:], g_ffn.to_broadcast([P, D])).then_inc(s_mc, 16)
                sp.dma_start(wr[:], w_router[0].rearrange("(k p) e -> p k e", p=P)).then_inc(s_mc, 16)
                sp.dma_start(brr[:], b_router.to_broadcast([P, NE])).then_inc(s_mc, 16)
                sp.dma_start(bdn[:], b_down[0]).then_inc(s_mc, 16)
                for i in range(NT):
                    if i >= 1:
                        sp.wait_ge(s_x2, 2 * i)
                    sp.dma_start(xr[:], x_rows[i * P:(i + 1) * P, :]).then_inc(s_xr, 16)
                for c in range(RAW):
                    load_chunk(sp, 6 + c, item_chunk(0, c))

            @block.gpsimd
            def _(pool):
                pool.iota(ioe[:], pattern=[[1, NE]], base=0, channel_multiplier=0,
                          allow_small_or_imprecise_dtypes=True).then_inc(s_io, 1)
                for i in range(NT):
                    pool.wait_ge(s_rv, RV * i + RV)
                    pool.dma_start(h2g_d[i * P:(i + 1) * P, :], h2r[i % 2][:]).then_inc(s_hs[i % 2], 16)
                    pool.wait_ge(s_ac, 2 * i + 2)
                    pool.dma_start(acc_d[i * P:(i + 1) * P, :], x2[i % 2][:]).then_inc(s_as[i % 2], 16)
                for s in range(2):
                    pool.wait_ge(s_hs[s], 16 * NT // 2)
                    pool.wait_ge(s_as[s], 16 * NT // 2)

            @block.scalar
            def _(act):
                act.wait_ge(s_mc, 80)

                def y_hi(i):
                    if i >= 2:
                        act.wait_ge(s_og, 2 * (i - 1))
                    tok = slice(i * P, (i + 1) * P)
                    act.activation(yh[i % 2][:, 0:4, :], ypool[:, :, tok], ACT.Copy).then_inc(s_yh, 1)
                    act.activation(yh[i % 2][:, 4:8, :], ya[:, :, tok], ACT.Copy).then_inc(s_yh, 1)

                y_hi(0)
                for p in range(8, 12):
                    split_hi(act, wh, p)
                y_hi(1)
                for i in range(NT):
                    if i + 2 < NT:
                        y_hi(i + 2)
                    act.wait_ge(s_x2, 2 * i + 2)
                    if i >= 2:
                        act.wait_ge(s_hs[i % 2], 16 * (i // 2))
                    act.activation(h2r[i % 2][:, 0:D], x2[i % 2][:], ACT.Square, accum_out=tiny[:, 3:4]).then_inc(s_ra, 1)
                    act.wait_ge(s_ra, 4 * i + 1)
                    act.activation(tiny[:, 4:5], tiny[:, 3:4], ACT.Sqrt, bias=epsb[:], scale=1.0 / D).then_inc(s_ra, 1)
                    for b in range(2):
                        act.wait_ge(s_tt, 2 * i + b + 1)
                        act.activation(h2t[:, 4 * b:4 * b + 4, :], psum[4 + b][:].rearrange("p (k t) -> p k t", k=4),
                                       ACT.Copy).then_inc(s_te, 1)
                    act.wait_ge(s_rv, RV * i + 4)
                    act.activation(ex[:], top8[:, 0:TOPK], ACT.Exp, bias=tiny[:, 0:1], accum_out=tiny[:, 1:2]).then_inc(s_ra, 2)
                    act.wait_ge(s_gt, i + 1)
                    act.activation(gtt[:], psum[6][0:NE, 256:256 + P], ACT.Copy).then_inc(s_ge, 1)

            @block.vector
            def _(dve):
                dve.wait_ge(s_mc, 80)
                dve.wait_ge(s_io, 1)

                def y_lo(i):
                    tok = slice(i * P, (i + 1) * P)
                    if i >= 1:
                        dve.wait_ge(s_og, 2 * i)
                    dve.wait_ge(s_yh, 2 * i + 2)
                    dve.tensor_tensor(yl[:, 0:4, :], ypool[:, :, tok], yh[i % 2][:, 0:4, :].bitcast(F32), ALU.subtract).then_inc(s_yl, 1)
                    dve.tensor_tensor(yl[:, 4:8, :], ya[:, :, tok], yh[i % 2][:, 4:8, :].bitcast(F32), ALU.subtract).then_inc(s_yl, 1)

                y_lo(0)
                for p in range(8, 12):
                    split_lo(dve, wh, wl, p)
                for i in range(NT):
                    n = RV * i
                    x2i, row = x2[i % 2], h2r[i % 2]
                    for half in range(2):
                        c = slice(half * 512, (half + 1) * 512)
                        dve.wait_ge(s_og, 2 * i + half + 1)
                        dve.wait_ge(s_xr, 16 * i + 16)
                        if i >= 2:
                            dve.wait_ge(s_as[i % 2], 16 * (i // 2))
                        dve.tensor_tensor(x2i[:, c], psum[2 * (i % 2) + half][:], xr[:, c], ALU.add).then_inc(s_x2, 1)
                    if i + 1 < NT:
                        y_lo(i + 1)
                    dve.wait_ge(s_ra, 4 * i + 2)
                    dve.reciprocal(tiny[:, 5:6], tiny[:, 4:5]).then_inc(s_rv, 1)
                    dve.wait_ge(s_rv, n + 1)
                    dve.scalar_tensor_tensor(out=row[:, 0:D], in0=x2i[:], scalar=tiny[:, 5:6], in1=gfr[:],
                                             op0=ALU.mult, op1=ALU.mult).then_inc(s_h2, 1)
                    dve.wait_ge(s_rl, i + 1)
                    dve.tensor_tensor(lg[:], psum[6][:, 0:NE], brr[:], ALU.add).then_inc(s_rv, 1)
                    dve.wait_ge(s_rv, n + 2)
                    dve.max(top8[:], lg[:]).then_inc(s_rv, 1)
                    dve.wait_ge(s_rv, n + 3)
                    dve.tensor_scalar(tiny[:, 0:1], top8[:, 0:1], -1.0, None, ALU.mult).then_inc(s_rv, 1)
                    dve.max_index(ix8[:], top8[:], lg[:]).then_inc(s_rv, 1)
                    dve.wait_ge(s_rv, n + 5)
                    dve.tensor_copy(ixf[:], ix8[:, 0:TOPK]).then_inc(s_rv, 1)
                    dve.wait_ge(s_rv, n + 6)
                    dve.tensor_tensor(ohe[:], ioe[:].unsqueeze(1).to_broadcast([P, TOPK, NE]),
                                      ixf[:].unsqueeze(2).to_broadcast([P, TOPK, NE]), ALU.is_equal).then_inc(s_rv, 1)
                    dve.wait_ge(s_ra, 4 * i + 4)
                    dve.reciprocal(tiny[:, 2:3], tiny[:, 1:2]).then_inc(s_rv, 1)
                    dve.wait_ge(s_rv, n + 8)
                    dve.tensor_scalar(gat[:], ex[:], tiny[:, 2:3], None, ALU.mult).then_inc(s_rv, 1)
                    dve.wait_ge(s_rv, n + 9)
                    dve.tensor_tensor(ohg[:], ohe[:], gat[:].unsqueeze(2).to_broadcast([P, TOPK, NE]), ALU.mult).then_inc(s_rv, 1)
                    with nc.allow_low_precision(reason="a sum of four values that are 0 or 1, one at most 1"):
                        dve.tensor_reduce(msk[:, i, :], ohe[:].rearrange("p j e -> p e j"), AX.X, ALU.add).then_inc(s_rv, 1)
                    dve.wait_ge(s_rv, n + 11)
                    dve.tensor_reduce(row[:, D:ROW], ohg[:].rearrange("p j e -> p e j"), AX.X, ALU.add).then_inc(s_rv, RV - 11)
                    for half in range(2):
                        c = slice(half * 512, (half + 1) * 512)
                        dve.wait_ge(s_bd, 2 * i + half + 1)
                        dve.tensor_tensor(x2i[:, c], psum[7][:], x2i[:, c], ALU.add).then_inc(s_ac, 1)

            @block.tensor
            def _(pe):
                pe.wait_ge(s_mc, 80)

                def out_proj(i):
                    pe.wait_ge(s_yl, 2 * i + 2)
                    for p in range(4):
                        pe.wait_ge(s_lo, 8 + p + 1)
                        if i >= 2 and p % 2 == 0:
                            pe.wait_ge(s_x2, 2 * (i - 2) + p // 2 + 1)
                        o = psum[2 * (i % 2) + p // 2][:, (p % 2) * HW_:(p % 2 + 1) * HW_]
                        for k in range(KT):
                            pe.matmul(o, yh[i % 2][:, k, :], wh[p][:, k, :], start=(k == 0), stop=False)
                            pe.matmul(o, yh[i % 2][:, k, :], wl[p][:, k, :], start=False, stop=False)
                            last = pe.matmul(o, yl[:, k, :], wh[p][:, k, :], start=False, stop=(k == KT - 1))
                        if p % 2 == 1:
                            last.then_inc(s_og, 1)

                def route(i):
                    pe.wait_ge(s_h2, i + 1)
                    for b in range(2):
                        if i >= 1:
                            pe.wait_ge(s_te, 2 * (i - 1) + b + 1)
                        for j in range(4):
                            k = 4 * b + j
                            last = pe.transpose(psum[4 + b][:, j * P:(j + 1) * P], h2r[i % 2][:, k * P:(k + 1) * P], ident[:])
                        last.then_inc(s_tt, 1)
                    pe.wait_ge(s_te, 2 * i + 2)
                    if i >= 1:
                        pe.wait_ge(s_ge, i)
                    for k in range(KT):
                        last = pe.matmul(psum[6][:, 0:NE], h2t[:, k, :], wr[:, k, :], start=(k == 0), stop=(k == KT - 1))
                    last.then_inc(s_rl, 1)

                def bias(i):
                    pe.wait_ge(s_rv, RV * i + RV)
                    pe.transpose(psum[6][0:NE, 256:256 + P], h2r[i % 2][:, D:ROW], ident[:]).then_inc(s_gt, 1)
                    pe.wait_ge(s_ge, i + 1)
                    for half in range(2):
                        pe.wait_ge(s_ac, 2 * i + half)
                        pe.matmul(psum[7][:], gtt[:], bdn[:, half * 512:(half + 1) * 512], start=True,
                                  stop=True).then_inc(s_bd, 1)

                for i in range(NT):
                    out_proj(i)
                    if i >= 1:
                        route(i - 1)
                        bias(i - 1)
                route(NT - 1)
                bias(NT - 1)
        if phases < 4:
            return

        m = phase("disp")
        m.end = nc.sbuf_usable_end // 32 * 32
        m.take("chosen_again", [P, NT, NE], BF16)
        posm = m.take("position", [P, NT, NE], F32)
        tab = m.take("item_table", [P, 3, ITEMS], I32)
        tbf = m.take("item_base", [P, ITEMS], F32)
        nit = m.take("item_count", [P, 1], I32)
        tok2 = m.take("token_id", [P, NT, 2], BF16)
        ios = m.take("iota_slot", [P, SLOTS], BF16)
        bup = m.take("b_up_t", [P, 2 * KT, NE], F32)
        moe_at = m.at
        tri = m.take("tri", [P, P], BF16)
        onb = m.take("ones_b", [P, P], BF16)
        trif = m.take("tri_f", [P, P], F32)
        onf = m.take("ones_ff", [P, P], F32)
        ioi = m.take("iota_item", [P, ITEMS], F32)
        bul = m.take("b_up_rows", [NE, 2 * D], F32)
        sm = m.take("small", [NE, 16], F32)
        ab = m.take("item_masks", [NE, 3, ITEMS], F32)
        ttmp = m.take("table_tmp", [P, 3, ITEMS], F32)
        s_dc = sem("disp_consts")
        s_dl = sem("disp_landed")
        s_dp = sem("disp_pe")
        s_dv = sem("disp_dve")
        BIGI = 4096

        with nc.Block() as block:
            @block.sync
            def _(sp):
                sp.dma_start(bul[:], b_up[0]).then_inc(s_dl, 16)

            @block.gpsimd
            def _(pool):
                pool.memset(onf[:], 1.0).then_inc(s_dc, 1)
                pool.memset(onb[:], 1.0).then_inc(s_dc, 1)
                pool.wait_ge(s_dc, 2)
                pool.affine_select(out=tri[:], in_=onb[:], pattern=[[1, P]], compare_op=ALU.is_gt, fill=0.0,
                                   base=0, channel_multiplier=-1).then_inc(s_dc, 1)
                pool.affine_select(out=trif[:], in_=onf[:], pattern=[[1, P]], compare_op=ALU.is_gt, fill=0.0,
                                   base=0, channel_multiplier=-1).then_inc(s_dc, 1)
                pool.iota(ioi[:], pattern=[[1, ITEMS]], base=0, channel_multiplier=0,
                          allow_small_or_imprecise_dtypes=True).then_inc(s_dc, 1)
                pool.iota(ios[:], pattern=[[1, SLOTS]], base=0, channel_multiplier=0,
                          allow_small_or_imprecise_dtypes=True).then_inc(s_dc, 1)
                pool.iota(tok2[:, :, 0:1], pattern=[[0, NT]], base=0, channel_multiplier=1,
                          allow_small_or_imprecise_dtypes=True).then_inc(s_dc, 1)
                pool.iota(tok2[:, :, 1:2], pattern=[[P, NT]], base=-BIGI, channel_multiplier=0,
                          allow_small_or_imprecise_dtypes=True).then_inc(s_dc, 1)

            @block.tensor
            def _(pe):
                pe.wait_ge(s_dc, 8)
                for i in range(NT):
                    o = psum[0][:, i * NE:(i + 1) * NE]
                    for j in range(i):
                        pe.matmul(o, onb[:], msk[:, j, :], start=(j == 0), stop=False)
                    last = pe.matmul(o, tri[:], msk[:, i, :], start=(i == 0), stop=True)
                last.then_inc(s_dp, 1)
                for i in range(NT):
                    last = pe.matmul(psum[1][0:NE, 0:1], msk[:, i, :], onb[:, 0:1], start=(i == 0), stop=(i == NT - 1))
                last.then_inc(s_dp, 1)
                pe.wait_ge(s_dl, 16)
                for t in range(2 * KT):
                    last = pe.transpose(psum[2][:, t * NE:(t + 1) * NE], bul[:, t * P:(t + 1) * P], ident[0:NE, 0:NE])
                last.then_inc(s_dp, 1)
                pe.wait_ge(s_dv, 8)
                pe.matmul(psum[3][0:NE, 0:1], trif[0:NE, 0:NE], sm[:, 1:2], start=True, stop=True).then_inc(s_dp, 1)
                pe.wait_ge(s_dv, 15)
                pe.matmul(psum[4][:, 0:3 * ITEMS], onf[0:NE, :], ab[:].rearrange("e a i -> e (a i)"), start=True, stop=True)
                pe.matmul(psum[4][:, 256:257], onf[0:NE, :], sm[:, 1:2], start=True, stop=True).then_inc(s_dp, 1)

            @block.vector
            def _(dve):
                step = [0]

                def done(ins):
                    step[0] += 1
                    ins.then_inc(s_dv, 1)
                    dve.wait_ge(s_dv, step[0])

                dve.wait_ge(s_dc, 8)
                dve.wait_ge(s_dp, 1)
                mk = msk[:].rearrange("p i e -> p (i e)")
                pm = posm[:].rearrange("p i e -> p (i e)")
                done(dve.scalar_tensor_tensor(out=pm, in0=psum[0][:, 0:NT * NE], scalar=1.0, in1=mk,
                                              op0=ALU.add, op1=ALU.mult))
                done(dve.tensor_scalar(pm, pm, -1.0, None, ALU.add))
                dve.wait_ge(s_dp, 2)
                done(dve.tensor_copy(sm[:, 0:1], psum[1][0:NE, 0:1]))
                done(dve.tensor_scalar(sm[:, 1:2], sm[:, 0:1], SLOTS + 0.5, 1.0, ALU.is_gt, ALU.add))
                src = 1
                for q in range(2, 6):
                    dst = src if q == 5 and False else (2 if src == 1 else 1)
                    done(dve.scalar_tensor_tensor(out=sm[:, dst:dst + 1], in0=sm[:, 0:1], scalar=q * SLOTS + 0.5,
                                                  in1=sm[:, src:src + 1], op0=ALU.is_gt, op1=ALU.add))
                    src = dst
                assert src == 1 and step[0] == 8
                dve.wait_ge(s_dp, 4)
                done(dve.tensor_copy(sm[:, 3:4], psum[3][0:NE, 0:1]))
                done(dve.tensor_tensor(sm[:, 4:5], sm[:, 3:4], sm[:, 1:2], ALU.add))
                done(dve.tensor_scalar(ab[:, 0, :], ioi[0:NE, :], sm[:, 3:4], None, ALU.is_ge))
                done(dve.tensor_scalar(ab[:, 1, :], ioi[0:NE, :], sm[:, 4:5], None, ALU.is_ge))
                done(dve.tensor_tensor(ab[:, 2, :], ab[:, 0, :], ab[:, 1, :], ALU.subtract))
                done(dve.tensor_scalar(ab[:, 2, :], ab[:, 2, :], sm[:, 0:1], None, ALU.mult))
                done(dve.tensor_scalar(ab[:, 1, :], ab[:, 1, :], sm[:, 1:2], None, ALU.mult))
                dve.wait_ge(s_dp, 5)
                done(dve.tensor_copy(ttmp[:], psum[4][:, 0:3 * ITEMS].rearrange("p (a i) -> p a i", a=3)))
                done(dve.tensor_copy(nit[:], psum[4][:, 256:257]))
                done(dve.tensor_scalar(tab[:, 0, :], ttmp[:, 0, :], -1.0, 0.0, ALU.add, ALU.max))
                done(dve.tensor_tensor(tbf[:], ioi[:], ttmp[:, 1, :], ALU.subtract))
                done(dve.tensor_scalar(tbf[:], tbf[:], float(SLOTS), None, ALU.mult))
                done(dve.tensor_tensor(tab[:, 1, :], ttmp[:, 2, :], tbf[:], ALU.subtract))
                dve.wait_ge(s_dp, 3)
                done(dve.tensor_copy(bup[:, 0:KT, :], psum[2][:, 0:KT * NE].rearrange("p (t e) -> p t e", t=KT)))
                done(dve.tensor_scalar(bup[:, KT:, :], psum[2][:, KT * NE:].rearrange("p (t e) -> p t e", t=KT),
                                       1.0, None, ALU.add))
        if phases < 5:
            return

        m = phase("moe")
        m.at = moe_at
        wh, wl = ring(m)
        xh = m.take("xg_hi", [P, KT, SLOTS], F32R)
        xl = m.take("xg_lo", [P, KT, SLOTS], F32R)
        rows = [m.take(f"xg_rows{b}", [P, ROW], F32) for b in range(2)]
        gl = m.take("glu", [P, 4, SLOTS], F32)
        sg = m.take("glu_sigmoid", [P, 4, SLOTS], F32)
        ln_ = m.take("lin", [P, 4, SLOTS], F32)
        tm = m.take("glu_lin", [P, 4, SLOTS], F32)
        hf = m.take("hidden", [P, 4, SLOTS], F32)
        uh = m.take("hidden_hi", [P, KT, SLOTS], F32R)
        ul = m.take("hidden_lo", [P, KT, SLOTS], F32R)
        yt = m.take("y_t", [P, KT, SLOTS], F32)
        yr = [m.take(f"y_rows{b}", [P, D], F32) for b in range(2)]
        sel = m.take("select", [P, NT, 2 * P], BF16)
        pcol = m.take("position_col", [P, NT], F32)
        ixs = m.take("row_index_sum", [P, 2], F32)
        ixn = m.take("row_index_next", [P, 2], U32)
        ixc = m.take("row_index_now", [P, 2], U32)
        gn = m.take("gate_next", [P, 2], F32)
        gc = m.take("gate_now", [P, 2], F32)
        BLK = (P, SLOTS - P)

        s_z = sem("moe_zeroed")
        s_pc = sem("position_col_done")
        s_sel = sem("select_done")
        s_ip = sem("index_product")
        s_is = sem("index_sum_done")
        s_ix = sem("index_done")
        s_rw = sem("rows_landed")
        s_xt = sem("x_transposed")
        s_xh = sem("x_hi_done")
        s_xl = sem("x_lo_done")
        s_gn = sem("gate_next_done")
        s_cur = sem("index_gate_now")
        s_evd = sem("up_evacuated")
        s_eva = sem("down_evacuated")
        s_sg = sem("sigmoid_done")
        s_tm = sem("glu_lin_done")
        s_hf = sem("hidden_done")
        s_uh = sem("hidden_hi_done")
        s_ul = sem("hidden_lo_done")
        s_yt = sem("y_transposed")
        s_ye = sem("y_rows_done")
        s_sc = sem("scatter_landed")
        s_sd = sem("scatters_done")

        GLU, LIN = (0, 2), (1, 3)

        with nc.Block() as block:
            def split_width(eng, n, f):
                with eng.If(n < WIDTHS[0] + 1):
                    f(WIDTHS[0])
                with eng.Else():
                    with eng.If(n < WIDTHS[1] + 1):
                        f(WIDTHS[1])
                    with eng.Else():
                        f(WIDTHS[2])

            @block.sync
            def _(sp):
                n_items = sp.value_load(nit[0:1, 0:1], min_val=NE, max_val=MAX_ITEMS)
                with sp.Fori(0, n_items) as i:
                    e = sp.value_load(tab[0:1, 0, bass.ds(i, 1)], min_val=0, max_val=NE - 1)
                    for c in range(RAW, NCH):
                        sp.wait_ge(s_lo, i * NPC + (PRO_PIECES + 2 * (c - RAW) + 2))
                        sp.dma_start(raw[c % RAW][:], item_chunk(e, c)).then_inc(s_raw[c % RAW], 16)
                    with sp.If(i + 1 < n_items):
                        e2 = sp.value_load(tab[0:1, 0, bass.ds(i + 1, 1)], min_val=0, max_val=NE - 1)
                        for c in range(RAW):
                            sp.wait_ge(s_lo, i * NPC + (PRO_PIECES + 2 * (c + RAW) + 2))
                            sp.dma_start(raw[c][:], item_chunk(e2, c)).then_inc(s_raw[c], 16)

            @block.gpsimd
            def _(pool):
                for b in range(2):
                    pool.memset(rows[b][:], 0.0).then_inc(s_z, 1)
                pool.memset(sel[:, :, SLOTS:], 0.0).then_inc(s_z, 1)
                pool.memset(yt[:], 0.0).then_inc(s_z, 1)
                n_items = pool.value_load(nit[0:1, 0:1], min_val=NE, max_val=MAX_ITEMS)

                rows_less_2, last_row = pool.alloc_register("rows_less_2"), pool.alloc_register("last_row")
                pool.reg_mov(rows_less_2, S - 2)

                def gather(i):
                    pool.wait_ge(s_ix, i + 1)
                    pool.reg_add(last_row, rows_less_2, 1)
                    for b in range(2):
                        pool.indirect_dma_start(out=rows[b][0:BLK[b], :], out_offset=None, in_=h2g_d,
                                                in_offset=bass.IndirectOffsetOnAxis(ap=ixn[0:BLK[b], b:b + 1], axis=0),
                                                bounds_check=last_row, oob_is_err=False).then_inc(s_rw, 16)

                pool.sem_inc(s_sd, 1)
                pool.wait_ge(s_z, 5)
                gather(0)
                with pool.Fori(0, n_items) as i:
                    with pool.If(i + 1 < n_items):
                        gather(i + 1)
                    pool.wait_ge(s_ye, 4 * i + 5)
                    pool.reg_add(last_row, rows_less_2, 1)
                    for b in range(2):
                        pool.indirect_dma_start(out=acc_d, out_offset=bass.IndirectOffsetOnAxis(ap=ixc[0:BLK[b], b:b + 1], axis=0),
                                                in_=yr[b][0:BLK[b], :], in_offset=None, bounds_check=last_row,
                                                oob_is_err=False, compute_op=ALU.add).then_inc(s_sc, 16)
                    pool.wait_ge(s_sc, i * 32 + 32)
                    pool.sem_inc(s_sd, 1)

            @block.scalar
            def _(act):
                act.sem_inc(s_eva, 2)
                act.sem_inc(s_ye, 1)
                n_items = act.value_load(nit[0:1, 0:1], min_val=NE, max_val=MAX_ITEMS)

                def hi(i, q):
                    slot = (q // 2) % RAW
                    act.wait_ge(s_raw[slot], i * 32 + (32 + 16 * (q // 2 // RAW + 1)))
                    if q >= RING:
                        act.wait_ge(s_pd, i * NPC + (q - RING + 1))
                    act.activation(wh[q % RING][:], raw[slot][:, :, (q % 2) * HW_:(q % 2 + 1) * HW_],
                                   ACT.Copy).then_inc(s_hi, 1)

                def x_hi(i):
                    for r in range(4):
                        act.wait_ge(s_xt, 4 * i + r + 1)
                        act.activation(xh[:, 2 * r:2 * r + 2, :],
                                       psum[4 + r][:, 0:2 * SLOTS].rearrange("p (k t) -> p k t", k=2),
                                       ACT.Copy).then_inc(s_xh, 1)

                def body(i, w, has_next):
                    for c in range(4):
                        hi(i, RING + 2 * c)
                        hi(i, RING + 2 * c + 1)
                        if c in GLU:
                            act.wait_ge(s_evd, 4 * i + c + 1)
                            act.activation(sg[:, :, 0:w], gl[:, :, 0:w], ACT.Sigmoid, scale=ALPHA).then_inc(s_sg, 1)
                        else:
                            act.wait_ge(s_hf, 2 * i + c // 2 + 2)
                            act.activation(uh[:, 4 * (c // 2):4 * (c // 2) + 4, 0:w], hf[:, :, 0:w], ACT.Copy).then_inc(s_uh, 1)

                def tail(i, w, c, has_next):
                    act.wait_ge(s_pd, i * NPC + 2 * c + 2)
                    if c == 4:
                        act.wait_ge(s_yt, 4 * i + 1)
                    for b in range(2):
                        last = act.activation(yt[:, 4 * (c - 4) + 2 * b:4 * (c - 4) + 2 * b + 2, 0:w],
                                              psum[2 * (c % 2) + b][:, 0:2 * w].rearrange("p (k t) -> p k t", k=2),
                                              ACT.Copy)
                    last.then_inc(s_eva, 1)

                def by_width(i, f):
                    n = act.value_load(tab[0:1, 1, bass.ds(i, 1)], min_val=0, max_val=S)
                    split_width(act, n, f)

                act.wait_ge(s_z, 5)
                for q in range(RING):
                    hi(0, q)
                x_hi(0)
                with act.Fori(0, n_items) as i:
                    by_width(i, lambda w: body(i, w, None))
                    with act.If(i + 1 < n_items):
                        x_hi(i + 1)
                        hi(i, NPC)
                        hi(i, NPC + 1)
                    by_width(i, lambda w: tail(i, w, 4, None))
                    with act.If(i + 1 < n_items):
                        hi(i, NPC + 2)
                        hi(i, NPC + 3)
                    by_width(i, lambda w: tail(i, w, 5, None))
                    for half in range(2):
                        for b in range(2):
                            act.wait_ge(s_yt, 4 * i + 2 * half + b + 2)
                            if half == 0 and b == 0:
                                act.wait_ge(s_sd, i + 1)
                                act.wait_ge(s_cur, i + 2)
                            act.activation(yr[b][0:BLK[b], half * 512:(half + 1) * 512],
                                           psum[4 + 2 * half + b][0:BLK[b], :], ACT.Copy,
                                           scale=gc[0:BLK[b], b:b + 1]).then_inc(s_ye, 1)

            @block.vector
            def _(dve):
                n_items = dve.value_load(nit[0:1, 0:1], min_val=NE, max_val=MAX_ITEMS)
                dve.sem_inc(s_cur, 1)
                dve.sem_inc(s_hf, 1)
                dve.memset(gn[:], 0.0).then_inc(s_z, 1)

                def position_col(i):
                    e = dve.value_load(tab[0:1, 0, bass.ds(i, 1)], min_val=0, max_val=NE - 1)
                    dve.wait_ge(s_ip, i + 1)
                    dve.tensor_scalar(pcol[:].unsqueeze(2), posm[:, :, bass.ds(e, 1)], tbf[:, bass.ds(i, 1)], None,
                                      ALU.subtract).then_inc(s_pc, 1)
                    dve.wait_ge(s_pc, i + 1)
                    for t in range(NT):
                        last = dve.tensor_scalar(sel[:, t, 0:SLOTS], ios[:], pcol[:, t:t + 1], None, ALU.is_equal)
                    last.then_inc(s_sel, 1)

                def index(i):
                    dve.wait_ge(s_ip, i + 2)
                    dve.tensor_scalar(ixs[:], psum[4][:, 0:4].rearrange("p (b a) -> p b a", a=2)[:, :, 0], float(BIGI), None,
                                      ALU.add).then_inc(s_is, 1)
                    dve.wait_ge(s_is, i + 1)
                    dve.tensor_tensor(ixn[:], ixs[:], psum[4][:, 0:4].rearrange("p (b a) -> p b a", a=2)[:, :, 1],
                                      ALU.add).then_inc(s_ix, 1)

                def lo(i, q):
                    slot = (q // 2) % RAW
                    dve.wait_ge(s_hi, i * NPC + (PRO_PIECES + q + 1))
                    dve.tensor_tensor(wl[q % RING][:], raw[slot][:, :, (q % 2) * HW_:(q % 2 + 1) * HW_],
                                      wh[q % RING][:].bitcast(F32), ALU.subtract).then_inc(s_lo, 1)

                def x_lo(i):
                    e = dve.value_load(tab[0:1, 0, bass.ds(i, 1)], min_val=0, max_val=NE - 1)
                    dve.wait_ge(s_rw, 32 * i + 32)
                    dve.wait_ge(s_cur, i + 1)
                    for b in range(2):
                        dve.tensor_copy(gn[0:BLK[b], b:b + 1], rows[b][0:BLK[b], bass.ds(e + D, 1)]).then_inc(s_gn, 1)
                    for r in range(4):
                        dve.wait_ge(s_xh, 4 * i + r + 1)
                        dve.tensor_tensor(xl[:, 2 * r:2 * r + 2, :],
                                          psum[4 + r][:, 0:2 * SLOTS].rearrange("p (k t) -> p k t", k=2),
                                          xh[:, 2 * r:2 * r + 2, :].bitcast(F32), ALU.subtract).then_inc(s_xl, 1)

                def evac(i, w, c, e):
                    dve.wait_ge(s_pd, i * NPC + 2 * c + 2)
                    part = c // 2
                    if c in GLU:
                        dve.wait_ge(s_hf, 2 * i + part + 1)
                        for t in range(4):
                            last = dve.tensor_scalar(gl[:, t, 0:w], psum[2 * (c % 2) + t // 2][:, (t % 2) * w:(t % 2 + 1) * w],
                                                     bup[:, 4 * part + t, bass.ds(e, 1)], LIMIT, ALU.add, ALU.min)
                        last.then_inc(s_evd, 1)
                        return
                    for t in range(4):
                        last = dve.tensor_scalar(ln_[:, t, 0:w], psum[2 * (c % 2) + t // 2][:, (t % 2) * w:(t % 2 + 1) * w],
                                                 bup[:, KT + 4 * part + t, bass.ds(e, 1)], LIMIT + 1.0, ALU.add, ALU.min)
                    last.then_inc(s_evd, 1)
                    dve.wait_ge(s_evd, 4 * i + c + 1)
                    dve.scalar_tensor_tensor(out=tm[:, :, 0:w], in0=ln_[:, :, 0:w], scalar=1.0 - LIMIT, in1=gl[:, :, 0:w],
                                             op0=ALU.max, op1=ALU.mult).then_inc(s_tm, 1)
                    dve.wait_ge(s_tm, 2 * i + part + 1)
                    dve.wait_ge(s_sg, 2 * i + part + 1)
                    dve.tensor_tensor(hf[:, :, 0:w], tm[:, :, 0:w], sg[:, :, 0:w], ALU.mult).then_inc(s_hf, 1)
                    dve.wait_ge(s_uh, 2 * i + part + 1)
                    dve.tensor_tensor(ul[:, 4 * part:4 * part + 4, 0:w], hf[:, :, 0:w],
                                      uh[:, 4 * part:4 * part + 4, 0:w].bitcast(F32), ALU.subtract).then_inc(s_ul, 1)

                def step(i, w, c, e):
                    lo(i, RING + 2 * c)
                    evac(i, w, c, e)
                    lo(i, RING + 2 * c + 1)

                dve.wait_ge(s_z, 5)
                position_col(0)
                index(0)
                for q in range(RING):
                    lo(0, q)
                x_lo(0)
                with dve.Fori(0, n_items) as i:
                    e = dve.value_load(tab[0:1, 0, bass.ds(i, 1)], min_val=0, max_val=NE - 1)
                    n = dve.value_load(tab[0:1, 1, bass.ds(i, 1)], min_val=0, max_val=S)
                    with dve.If(i + 1 < n_items):
                        position_col(i + 1)
                    split_width(dve, n, lambda w: step(i, w, 0, e))
                    dve.wait_ge(s_sd, i + 1)
                    dve.wait_ge(s_ye, 4 * i + 1)
                    dve.wait_ge(s_gn, 2 * i + 2)
                    dve.wait_ge(s_ix, i + 1)
                    dve.tensor_copy(ixc[:], ixn[:])
                    dve.tensor_copy(gc[:], gn[:]).then_inc(s_cur, 1)
                    with dve.If(i + 1 < n_items):
                        index(i + 1)

                    def rest(w):
                        for c in range(1, 4):
                            step(i, w, c, e)

                    split_width(dve, n, rest)
                    with dve.If(i + 1 < n_items):
                        x_lo(i + 1)
                        for q in range(NPC, NPC + RING):
                            lo(i, q)

            @block.tensor
            def _(pe):
                n_items = pe.value_load(nit[0:1, 0:1], min_val=NE, max_val=MAX_ITEMS)

                def index_product(i):
                    pe.wait_ge(s_sel, i + 1)
                    for b in range(2):
                        for t in range(NT):
                            last = pe.matmul(psum[4][:, 2 * b:2 * b + 2], sel[:, t, b * P:(b + 1) * P], tok2[:, t, :],
                                             start=(t == 0), stop=(t == NT - 1))
                    last.then_inc(s_ip, 1)

                def x_transposes(i):
                    pe.wait_ge(s_rw, 32 * i + 32)
                    pe.wait_ge(s_ix, i + 1)
                    for r in range(4):
                        for j in range(2):
                            k = 2 * r + j
                            pe.transpose(psum[4 + r][:, j * SLOTS:j * SLOTS + P], rows[0][:, k * P:(k + 1) * P], ident[:])
                            last = pe.transpose(psum[4 + r][:, j * SLOTS + P:(j + 1) * SLOTS],
                                                rows[1][0:BLK[1], k * P:(k + 1) * P], ident[0:BLK[1], 0:BLK[1]])
                        last.then_inc(s_xt, 1)

                def group(i, w, c):
                    sh, sl_ = (xh, xl) if c < 4 else (uh, ul)
                    if c == 0:
                        pe.wait_ge(s_eva, 2 * i + 1)
                        pe.wait_ge(s_xl, 4 * i + 4)
                    elif c == 1:
                        pe.wait_ge(s_eva, 2 * i + 2)
                    else:
                        pe.wait_ge(s_evd, 4 * i + c - 1)
                    for a in range(2):
                        q = 2 * c + a
                        pe.wait_ge(s_lo, i * NPC + (PRO_PIECES + q + 1))
                        for t in range(2):
                            o = psum[2 * (c % 2) + a][:, t * w:(t + 1) * w]
                            f = slice(t * P, (t + 1) * P)
                            for k in range(KT):
                                if c == 4 and a == 0 and t == 0 and k % 4 == 0:
                                    pe.wait_ge(s_ul, 2 * i + k // 4 + 1)
                                pe.matmul(o, wh[q % RING][:, k, f], sh[:, k, 0:w], start=(k == 0), stop=False)
                                pe.matmul(o, wh[q % RING][:, k, f], sl_[:, k, 0:w], start=False, stop=False)
                                last = pe.matmul(o, wl[q % RING][:, k, f], sh[:, k, 0:w], start=False, stop=(k == KT - 1))
                        last.then_inc(s_pd, 1)

                pe.sem_inc(s_ip, 1)
                pe.sem_inc(s_yt, 1)
                pe.wait_ge(s_z, 5)
                index_product(0)
                x_transposes(0)
                with pe.Fori(0, n_items) as i:
                    n = pe.value_load(tab[0:1, 1, bass.ds(i, 1)], min_val=0, max_val=S)

                    def up(cs):
                        def f(w):
                            for c in cs:
                                group(i, w, c)
                        return f

                    split_width(pe, n, up((0, 1)))
                    with pe.If(i + 1 < n_items):
                        pe.wait_ge(s_ye, 4 * i + 1)
                        index_product(i + 1)
                    split_width(pe, n, up((2, 3)))
                    with pe.If(i + 1 < n_items):
                        x_transposes(i + 1)
                    split_width(pe, n, up((4, 5)))
                    with pe.If(i + 1 < n_items):
                        pe.wait_ge(s_xl, 4 * i + 8)
                    pe.wait_ge(s_ye, 4 * i + 1)
                    pe.wait_ge(s_eva, 2 * i + 4)
                    for half in range(2):
                        for b in range(2):
                            for j in range(4):
                                k = 4 * half + j
                                last = pe.transpose(psum[4 + 2 * half + b][0:BLK[b], j * P:(j + 1) * P],
                                                    yt[:, k, b * P:b * P + BLK[b]], ident[:])
                            last.then_inc(s_yt, 1)

        m = phase("fin")
        ac = [m.take(f"acc{i}", [P, D], F32) for i in range(NT)]
        oo = [m.take(f"out{i}", [P, D], F32) for i in range(NT)]
        gfin = m.take("g_final_row", [P, D], F32)
        dump = m.take("final_dump", [P, D], BF16)
        fs = m.take("final_small", [P, 3 * NT], F32)
        s_fl = [sem(f"acc_landed{i}") for i in range(NT)]
        s_fa2 = sem("final_act")
        s_fr = sem("final_recip")
        s_fo = sem("final_rows")
        s_fs = sem("final_stored")
        s_gf = sem("g_final_landed")
        with nc.Block() as block:
            @block.sync
            def _(sp):
                for i in range(NT):
                    sp.dma_start(ac[i][:], acc_d[i * P:(i + 1) * P, :]).then_inc(s_fl[i], 16)
                    if i == 0:
                        sp.dma_start(gfin[:], g_final.unsqueeze(0).to_broadcast([P, D])).then_inc(s_gf, 16)
                for i in range(NT):
                    sp.wait_ge(s_fo, i + 1)
                    sp.dma_start(out_rows[i * P:(i + 1) * P, :], oo[i][:]).then_inc(s_fs, 16)
                sp.wait_ge(s_fs, 16 * NT)

            @block.scalar
            def _(act):
                for i in range(NT):
                    act.wait_ge(s_fl[i], 16)
                    if i >= 1:
                        act.wait_ge(s_fa2, 2 * i)
                    act.activation(dump[:], ac[i][:], ACT.Square, accum_out=fs[:, i:i + 1]).then_inc(s_fa2, 1)
                    act.wait_ge(s_fa2, 2 * i + 1)
                    act.activation(fs[:, NT + i:NT + i + 1], fs[:, i:i + 1], ACT.Sqrt, bias=epsb[:], scale=1.0 / D).then_inc(s_fa2, 1)

            @block.vector
            def _(dve):
                dve.wait_ge(s_gf, 16)
                for i in range(NT):
                    dve.wait_ge(s_fa2, 2 * i + 2)
                    dve.reciprocal(fs[:, 2 * NT + i:2 * NT + i + 1], fs[:, NT + i:NT + i + 1]).then_inc(s_fr, 1)
                    dve.wait_ge(s_fr, i + 1)
                    dve.scalar_tensor_tensor(out=oo[i][:], in0=ac[i][:], scalar=fs[:, 2 * NT + i:2 * NT + i + 1],
                                             in1=gfin[:], op0=ALU.mult, op1=ALU.mult).then_inc(s_fo, 1)


_INS = ["x", "g_mix", "w_in", "b_forget", "w_pool", "pool_scale", "w_out", "g_ffn", "w_router", "b_router",
        "w_up", "b_up", "w_down", "b_down", "g_final"]


def kernel(**inputs):
    import concourse.bacc as bacc
    from concourse.bass_utils import run_bass_kernel_spmd

    nc = bacc.Bacc("TRN2", target_bir_lowering=False, num_devices=1)
    arrays, args = {}, []
    for name in _INS + ["identity"]:
        a = np.eye(P, dtype=np.float32) if name == "identity" else np.ascontiguousarray(inputs[name])
        arrays[f"in_{name}"] = a
        args.append(nc.dram_tensor(f"in_{name}", a.shape, mybir.dt.from_np(a.dtype), kind="ExternalInput").ap())
    args.append(nc.dram_tensor("out_0", (1, S, D), F32, kind="ExternalOutput").ap())
    build(nc, *args)
    r = run_bass_kernel_spmd(nc, [arrays], core_ids=[0])
    return r.results[0]["out_0"]
```

```python
from contextlib import ExitStack

import numpy as np
import concourse.bass as bass
from concourse import mybir

F32 = mybir.dt.float32
F32R = mybir.dt.float32r
BF16 = mybir.dt.bfloat16
I32 = mybir.dt.int32
U32 = mybir.dt.uint32
ALU = mybir.AluOpType
ACT = mybir.ActivationFunctionType
AX = mybir.AxisListType

P = 128
D = 1024
S = 1024
KT = D // P
NT = S // P
PW = 512
NG = 4
PAD = 16
AW = 512
HD = 64
NH = AW // HD
NE = 32
TOPK = 4
EPS = 1e-5
LIMIT = 7.0
ALPHA = 1.702
NEG = -1.0e30

CW = 512
NCH = 6
SLOTS = 192
MAX_ITEMS = 53
ITEMS = 56
WIDTHS = (128, 136, 144, 152, 160, 176, SLOTS)
ROW = D + NE


class Map:

    def __init__(self, nc, at, end):
        self.nc, self.at, self.end = nc, at, end

    def take(self, name, shape, dt, at=None):
        size = 1
        for n in shape[1:]:
            size *= n
        size *= 2 if dt == BF16 else 4
        off = self.at if at is None else at
        if at is None:
            self.at += (size + 31) // 32 * 32
            assert self.at <= self.end, (name, self.at, self.end)
        return self.nc.alloc_sbuf_tensor_at(name, shape, dt, offset=off)


def build(nc, x, g_mix, w_in, b_forget, w_pool, pool_scale, w_out, g_ffn, w_router, b_router,
          w_up, b_up, w_down, b_down, g_final, ident_in, out, phases=9, dbg=None):
    ctx = ExitStack()
    with ctx:
        def sem(name):
            return ctx.enter_context(nc.semaphore(name))

        x_rows = x.rearrange("b s d -> (b s) d")
        out_rows = out.rearrange("b s d -> (b s) d")

        qk_d = nc.dram_tensor("qk_d", [2, AW, S], F32).ap()
        v_d = nc.dram_tensor("v_d", [S, AW], F32).ap()
        negc_d = nc.dram_tensor("negc_d", [NH, S], F32).ap()
        yp_d = nc.dram_tensor("yp_d", [PW, S], F32).ap()
        h2g_d = nc.dram_tensor("h2g_d", [S, ROW], F32).ap()
        acc_d = nc.dram_tensor("acc_d", [S, D], F32).ap()

        keep = Map(nc, (nc.sbuf_base + 31) // 32 * 32, nc.sbuf_usable_end)
        raw_at = keep.at
        raw = [keep.take(f"weights{i}", [P, KT, CW], F32) for i in range(NCH)]
        raw_r = {i: keep.take(f"weights{i}_r", [P, KT, CW], F32R, at=raw_at + 4 * KT * CW * i) for i in (4, 5)}
        ident = keep.take("ident", [P, P], F32)
        identb = keep.take("identb", [P, P], BF16)
        one = keep.take("one", [P, 1], F32)
        epsb = keep.take("eps", [P, 1], F32)
        top = keep.at
        end = nc.sbuf_usable_end // 32 * 32

        def phase():
            return Map(nc, top, end)

        ps = ctx.enter_context(nc.psum_tensor("ps", [P, 8 * 512], F32))
        psum = [ps[:, i * 512:(i + 1) * 512] for i in range(8)]
        psum2 = [ps[:, i * 1024:(i + 1) * 1024] for i in range(4)]

        s_raw = [sem(f"chunk_landed{i}") for i in range(NCH)]
        s_pd = sem("item_chunk_used")

        def cols(w, c0, n=CW):
            return w[:, c0:c0 + n].rearrange("(k p) n -> p k n", p=P)

        def item_chunk(e, c):
            w, c0 = (w_up, (0, D, CW, D + CW)[c]) if c < 4 else (w_down, (c - 4) * CW)
            return w[0, bass.ds(e, 1), :, c0:c0 + CW].rearrange("e (k p) n -> p (e k) n", p=P)

        w_in0 = w_in[0]
        w_out0 = w_out[0]
        pro_chunks = [cols(w_in0, PW + 2 * AW), cols(w_in0, 0), cols(w_in0, PW), cols(w_in0, PW + AW),
                      cols(w_out0, 0), cols(w_out0, CW)]

        m = Map(nc, end - 4 * 4 * S - 2 * P, end)
        QC = [m.take(f"q_rows{i}", [P, S], F32) for i in range(2)]
        KC = [m.take(f"k_rows{i}", [P, S], F32) for i in range(2)]
        maskb = m.take("mask", [P, P], BF16)
        s_on = sem("attn_consts")
        attn_end = end - 4 * 4 * S - 2 * P

        m = phase()
        m.end = attn_end
        hT = m.take("h_t", [P, KT, S], F32)
        x_at = m.at
        xt = [m.take(f"xt{i}", [P, D], F32) for i in range(2)]
        xn = [m.take(f"xn{i}", [P, D], F32) for i in range(2)]
        fz, fabs, fln, negc = [m.take(f"forget_{s}", [NH, S], F32, at=x_at + 4 * D * i)
                               for i, s in enumerate(("z", "abs", "ln", "neg_c"))]
        grow = m.take("g_mix_row", [P, D], F32)
        ubuf = [m.take(f"u{i}", [P, PAD + S], F32) for i in range(2)]
        usum = [m.take(f"u_sum{i}", [P, PAD + S], F32) for i in range(2)]
        pout = [m.take(f"pool_out{i}", [P, S], F32) for i in range(2)]
        stage = [m.take(f"stage{i}", [P, 512], F32) for i in range(4)]
        wp = m.take("w_pool_sb", [P, NG, P], F32)
        wf = m.take("w_f", [P, KT, NH], F32)
        psc = m.take("pool_scale_col", [P, NG], F32)
        bfc = m.take("b_forget_col", [NH, 1], F32)
        rc = m.take("rcount", [P, PAD], F32)
        sqj = m.take("square_dump", [P, D], BF16)
        ssq = m.take("ssq", [P, NT], F32)
        rst = m.take("rstd", [P, 2 * NT], F32)

        N_V, N_U, N_Q, GRP = 0, NT, NT + 8, NT + 24
        s_x = [sem(f"x_landed{i}") for i in range(2)]
        s_c = sem("proj_consts")
        s_c2 = sem("pool_consts")
        s_sq = sem("x_squares")
        s_eps = sem("eps_set")
        s_rs = sem("x_rstd")
        s_xn = sem("x_normed")
        s_tr = sem("h_transposed")
        s_he = [sem(f"h_t_half{i}_done") for i in range(2)]
        s_g = sem("proj_group")
        s_ge = [sem("proj_even_evacuated"), sem("proj_odd_evacuated")]
        s_st = [sem(f"proj_stored{i}") for i in range(4)]
        s_f = sem("forget_logits")
        s_fv = sem("forget_dve")
        s_fa = sem("forget_act")
        s_fx = sem("neg_log_f_done")
        s_nc = sem("neg_c_stored")
        s_rc = sem("rcount_set")
        s_uv = sem("pool_dve")
        s_pm = sem("pool_product")
        s_pe = sem("pool_evacuated")
        s_ps = [sem(f"pool_stored{i}") for i in range(2)]
        s_id = sem("identity_bf16")

        POOL_DONE = []
        count = 4
        for g in range(NG):
            count += (g + 1) + 3
            POOL_DONE.append(count)

        with nc.Block() as block:
            def store(sp, n, slot):
                sp.wait_ge(s_ge[n % 2], n // 2 + 1)
                if n < N_U:
                    dst = v_d[n * P:(n + 1) * P, :]
                else:
                    ft, half = divmod(n - N_Q, 2)
                    dst = qk_d[ft // 4, (ft % 4) * P:(ft % 4 + 1) * P, half * 512:half * 512 + 512]
                sp.dma_start(dst, stage[slot % 4][:]).then_inc(s_st[slot % 4], 16)

            @block.sync
            def _(sp):
                sp.dma_start(xt[0][:], x_rows[0:P, :]).then_inc(s_x[0], 16)
                sp.dma_start(ident[:], ident_in).then_inc(s_c, 16)
                sp.dma_start(grow[:], g_mix.to_broadcast([P, D])).then_inc(s_c, 16)
                sp.dma_start(xt[1][:], x_rows[P:2 * P, :]).then_inc(s_x[1], 16)
                sp.dma_start(raw[0][:], pro_chunks[0]).then_inc(s_raw[0], 16)
                for i in range(2, NT):
                    sp.wait_ge(s_xn, i - 1)
                    sp.dma_start(xt[i % 2][:], x_rows[i * P:(i + 1) * P, :]).then_inc(s_x[i % 2], 16)
                    if i >= 3:
                        store(sp, i - 3, i - 3)
                sp.dma_start(wf[:], cols(w_in0, PW + 3 * AW, NH)).then_inc(s_c2, 16)
                sp.dma_start(bfc[:], b_forget.rearrange("o h -> h o"), allow_slow_non_contiguous=True).then_inc(s_c2, 16)
                sp.dma_start(psc[:], pool_scale[0].rearrange("(g p) -> p g", p=P),
                             allow_slow_non_contiguous=True).then_inc(s_c2, 16)
                sp.dma_start(wp[:], w_pool[0].rearrange("g c d -> c g d")).then_inc(s_c2, 16)
                sp.dma_start(raw[1][:], pro_chunks[1]).then_inc(s_raw[1], 16)
                for n in range(NT - 3, NT):
                    store(sp, n, n)
                for n in range(2, NCH):
                    sp.dma_start(raw[n][:], pro_chunks[n]).then_inc(s_raw[n], 16)
                for n in range(N_Q, GRP):
                    store(sp, n, n - 8)

            @block.gpsimd
            def _(pool):
                pool.memset(epsb[:], EPS).then_inc(s_eps, 1)
                pool.memset(one[:], 1.0).then_inc(s_eps, 1)
                for t in range(PAD):
                    pool.memset(rc[:, t:t + 1], 1.0 / (t + 1)).then_inc(s_rc, 1)

                pool.wait_ge(s_rc, PAD)
                for s in range(2):
                    pool.memset(KC[s][HD:P], 0.0).then_inc(s_on, 1)
                    pool.wait_ge(s_on, 3 * s + 1)
                    pool.memset(QC[s][HD:P], 0.0).then_inc(s_on, 1)
                    pool.wait_ge(s_on, 3 * s + 2)
                    pool.memset(QC[s][HD:HD + 1], 1.0).then_inc(s_on, 1)
                    pool.wait_ge(s_on, 3 * s + 3)
                pool.memset(maskb[:], 0.0).then_inc(s_on, 1)
                pool.wait_ge(s_on, 7)
                pool.affine_select(out=maskb[:], in_=maskb[:], pattern=[[-1, P]], compare_op=ALU.is_ge,
                                   fill=NEG, base=0, channel_multiplier=1).then_inc(s_on, 1)

                for g in range(NG):
                    pool.wait_ge(s_pe, 2 * g + 2)
                    pool.dma_start(yp_d[g * P:(g + 1) * P, :], pout[g % 2][:]).then_inc(s_ps[g % 2], 16)
                pool.wait_ge(s_ps[0], 16 * NG // 2)
                pool.wait_ge(s_ps[1], 16 * NG // 2)

            def evac(eng, n):
                eng.wait_ge(s_g, n + 1)
                if N_U <= n < N_Q:
                    g, half = divmod(n - N_U, 2)
                    if g >= 2:
                        eng.wait_ge(s_uv, POOL_DONE[g - 2])
                    dst = ubuf[g % 2][:, PAD + half * 512:PAD + half * 512 + 512]
                else:
                    slot = n if n < N_U else n - 8
                    if slot >= 4:
                        eng.wait_ge(s_st[slot % 4], 16 * (slot // 4))
                    dst = stage[slot % 4][:]
                scale = HD ** -0.5 if N_Q <= n < N_Q + 8 else 1.0
                if n % 2 == 0:
                    eng.activation(dst, psum[n % 4][:], ACT.Copy, scale=scale).then_inc(s_ge[0], 1)
                else:
                    eng.tensor_scalar(dst, psum[n % 4][:], scale, None, ALU.mult).then_inc(s_ge[1], 1)

            @block.scalar
            def _(act):
                act.wait_ge(s_eps, 2)

                def squares(i):
                    act.wait_ge(s_x[i % 2], 16 * (i // 2 + 1))
                    if i >= 1:
                        act.wait_ge(s_sq, 2 * i)
                    act.activation(sqj[:], xt[i % 2][:], ACT.Square, accum_out=ssq[:, i:i + 1]).then_inc(s_sq, 1)
                    act.wait_ge(s_sq, 2 * i + 1)
                    act.activation(rst[:, i:i + 1], ssq[:, i:i + 1], ACT.Sqrt, bias=epsb[:],
                                   scale=1.0 / D).then_inc(s_sq, 1)

                squares(0)
                for i in range(NT):
                    if i + 1 < NT:
                        squares(i + 1)
                    act.wait_ge(s_tr, 2 * i + 1)
                    act.activation(hT[:, 0:4, i * P:(i + 1) * P],
                                   psum[4][:].rearrange("p (k t) -> p k t", k=4), ACT.Copy).then_inc(s_he[0], 1)
                    if i % 2 == 1:
                        evac(act, i - 1)
                act.wait_ge(s_c, 32)
                act.activation(identb[:], ident[:], ACT.Copy).then_inc(s_id, 1)
                act.wait_ge(s_fv, 3)
                act.activation(fln[:], fabs[:], ACT.Exp, scale=-1.0).then_inc(s_fa, 1)
                act.wait_ge(s_fa, 1)
                act.activation(fln[:], fln[:], ACT.Ln, bias=one[0:NH, :]).then_inc(s_fa, 1)

                def pool_out(g):
                    for half in range(2):
                        act.wait_ge(s_pm, 2 * g + half + 1)
                        if g >= 2 and half == 0:
                            act.wait_ge(s_ps[g % 2], 16 * (g // 2))
                        act.activation(pout[g % 2][:, half * 512:half * 512 + 512], psum[6 + half][:], ACT.Copy,
                                       scale=psc[:, g:g + 1]).then_inc(s_pe, 1)

                act.wait_ge(s_c2, 64)
                for n in range(N_U, GRP, 2):
                    evac(act, n)
                    if n >= N_U + 4 and (n - N_U - 4) // 2 < NG:
                        pool_out((n - N_U - 4) // 2)
                act.wait_ge(s_fv, 5)
                act.dma_start(negc_d, negc[:]).then_inc(s_nc, 16)
                act.wait_ge(s_nc, 16)

            @block.vector
            def _(dve):
                dve.wait_ge(s_c, 32)
                for i in range(NT):
                    dve.wait_ge(s_sq, 2 * i + 2)
                    dve.reciprocal(rst[:, NT + i:NT + i + 1], rst[:, i:i + 1]).then_inc(s_rs, 1)
                    dve.wait_ge(s_rs, i + 1)
                    if i >= 2:
                        dve.wait_ge(s_tr, 2 * (i - 2) + 2)
                    dve.scalar_tensor_tensor(out=xn[i % 2][:], in0=xt[i % 2][:], scalar=rst[:, NT + i:NT + i + 1],
                                             in1=grow[:], op0=ALU.mult, op1=ALU.mult).then_inc(s_xn, 1)
                    dve.wait_ge(s_tr, 2 * i + 2)
                    dve.tensor_copy(hT[:, 4:8, i * P:(i + 1) * P],
                                    psum[5][:].rearrange("p (k t) -> p k t", k=4)).then_inc(s_he[1], 1)
                    if i % 2 == 0 and i >= 2:
                        evac(dve, i - 1)
                evac(dve, NT - 1)
                for t, b in enumerate(ubuf + usum):
                    dve.memset(b[:, 0:PAD], 0.0).then_inc(s_uv, 1)
                dve.wait_ge(s_c2, 64)
                for half in range(2):
                    dve.wait_ge(s_f, half + 1)
                    dve.tensor_scalar(fz[:, half * 512:half * 512 + 512], psum[6 + half][0:NH, :], bfc[:], None,
                                      ALU.add).then_inc(s_fv, 1)
                dve.wait_ge(s_fv, 2)
                dve.scalar_tensor_tensor(out=fabs[:], in0=fz[:], scalar=-1.0, in1=fz[:],
                                         op0=ALU.mult, op1=ALU.max).then_inc(s_fv, 1)

                def forget_cumulate():
                    dve.wait_ge(s_fa, 2)
                    dve.scalar_tensor_tensor(out=fabs[:], in0=fz[:], scalar=0.0, in1=fln[:],
                                             op0=ALU.min, op1=ALU.subtract).then_inc(s_fv, 1)
                    dve.wait_ge(s_fv, 4)
                    dve.tensor_scalar(fln[:], fabs[:], -1.0, None, ALU.mult).then_inc(s_fx, 1)
                    dve.wait_ge(s_fx, 1)
                    dve.tensor_tensor_scan(negc[:], fln[:], fln[:], 0.0, ALU.add, ALU.max).then_inc(s_fv, 1)

                dve.wait_ge(s_rc, PAD)
                cnt = 4
                for g in range(NG):
                    evac(dve, N_U + 2 * g + 1)
                    u = ubuf[g % 2]
                    dve.wait_ge(s_ge[0], (N_U + 2 * g) // 2 + 1)
                    dve.wait_ge(s_ge[1], (N_U + 2 * g) // 2 + 1)
                    if g == 0:
                        dve.wait_ge(s_uv, 4)
                    src, w = u, 1
                    for lev in range(g + 1):
                        dst = usum[lev % 2]
                        if lev >= 1:
                            dve.wait_ge(s_uv, cnt)
                        elif g >= 1:
                            dve.wait_ge(s_pm, 2 * g)
                        dve.tensor_tensor(dst[:, PAD:], src[:, PAD:], src[:, PAD - w:PAD + S - w],
                                          ALU.add).then_inc(s_uv, 1)
                        cnt += 1
                        src, w = dst, 2 * w
                    other = usum[(g + 1) % 2]
                    dve.wait_ge(s_uv, cnt)
                    dve.scalar_tensor_tensor(out=other[:, PAD:], in0=src[:, PAD:], scalar=1.0 / w,
                                             in1=u[:, PAD:], op0=ALU.mult, op1=ALU.subtract).then_inc(s_uv, 1)
                    cnt += 1
                    dve.wait_ge(s_uv, cnt)
                    dve.tensor_tensor(src[:, PAD:PAD + w - 1], src[:, PAD:PAD + w - 1], rc[:, 0:w - 1], ALU.mult).then_inc(s_uv, 1)
                    cnt += 1
                    dve.wait_ge(s_uv, cnt)
                    dve.tensor_tensor(other[:, PAD:PAD + w - 1], src[:, PAD:PAD + w - 1],
                                      u[:, PAD:PAD + w - 1], ALU.subtract).then_inc(s_uv, 1)
                    cnt += 1
                    assert cnt == POOL_DONE[g]
                for n in range(N_Q + 1, GRP, 2):
                    evac(dve, n)
                    if n == N_Q + 3:
                        forget_cumulate()

            @block.tensor
            def _(pe):
                pe.wait_ge(s_c, 32)

                def bank_free(n):
                    if n >= 4:
                        pe.wait_ge(s_ge[n % 2], (n - 4) // 2 + 1)

                def v_group(i):
                    bank_free(i)
                    if i == 0:
                        pe.wait_ge(s_raw[0], 16)
                    pe.wait_ge(s_he[0], i + 1)
                    pe.wait_ge(s_he[1], i + 1)
                    for k in range(KT):
                        last = pe.matmul(psum[i % 4][:], hT[:, k, i * P:(i + 1) * P], raw[0][:, k, :],
                                         start=(k == 0), stop=(k == KT - 1))
                    last.then_inc(s_g, 1)

                def pool_product(g):
                    pe.wait_ge(s_uv, POOL_DONE[g])
                    if g == 0:
                        pe.wait_ge(s_fv, 2)
                    p = usum[(g + 1) % 2]
                    for half in range(2):
                        if g >= 1:
                            pe.wait_ge(s_pe, 2 * (g - 1) + half + 1)
                        pe.matmul(psum[6 + half][:], wp[:, g, :], p[:, PAD + half * 512:PAD + half * 512 + 512],
                                  start=True, stop=True).then_inc(s_pm, 1)

                for i in range(NT):
                    pe.wait_ge(s_xn, i + 1)
                    for b in range(2):
                        if i >= 1:
                            pe.wait_ge(s_he[b], i)
                        for j in range(4):
                            k = 4 * b + j
                            last = pe.transpose(psum[4 + b][:, j * P:(j + 1) * P], xn[i % 2][:, k * P:(k + 1) * P], ident[:])
                        last.then_inc(s_tr, 1)
                    if i >= 1:
                        v_group(i - 1)
                v_group(NT - 1)
                pe.wait_ge(s_c2, 64)
                for half in range(2):
                    for k in range(KT):
                        last = pe.matmul(psum[6 + half][0:NH, :], wf[:, k, :], hT[:, k, half * 512:half * 512 + 512],
                                         start=(k == 0), stop=(k == KT - 1))
                    last.then_inc(s_f, 1)
                for n in range(N_U, GRP):
                    c, (t, half) = 1 + (n - N_U) // 8, divmod((n - N_U) % 8, 2)
                    if t == 0 and half == 0:
                        pe.wait_ge(s_raw[c], 16)
                    bank_free(n)
                    for k in range(KT):
                        last = pe.matmul(psum[n % 4][:], raw[c][:, k, t * P:(t + 1) * P],
                                         hT[:, k, half * 512:half * 512 + 512], start=(k == 0), stop=(k == KT - 1))
                    last.then_inc(s_g, 1)
                    if half == 1 and n >= N_U + 5 and (n - N_U - 5) // 2 < NG:
                        pool_product((n - N_U - 5) // 2)


        if phases < 2:
            return

        m = phase()
        m.end = attn_end
        ya = m.take("y_attn", [P, 4, S], F32)
        mix_at = m.at
        VH = [m.take(f"v_head{i}", [P, NT, HD], F32) for i in range(2)]
        prb = [m.take(f"prob_big{i}", [P, S], F32) for i in range(2)]
        prs = [m.take(f"prob_small{i}", [P, 512], F32) for i in range(2)]
        pt = [[m.take(f"prob_t{h}{g}", [P, 2 * g + 2, 2 * P], F32) for g in range(4)] for h in range(2)]
        nmx = m.take("neg_max", [P, 16], F32)
        rsm = m.take("row_sum", [P, 16], F32)
        rrs = m.take("row_sum_inv", [P, 16], F32)

        ypool = m.take("y_pool", [P, 4, S], F32)
        gfr = m.take("g_ffn_row", [P, D], F32)
        mix_end = m.at - 4 * (4 * S + D)
        s_mc = sem("mix_consts")

        QT = 2 * NT
        ORDER = (7, 0, 6, 1, 5, 2, 4, 3)
        TB = 3 * NT
        PRODUCT_AT = {4: 3, 5: 0, 8: 2, 9: 1}
        NPROD = 8
        s_ld = [sem(f"head_landed{i}") for i in range(2)]
        s_S = sem("logits")
        s_nm = sem("neg_max_done")
        s_P = sem("exp_done")
        s_rr = sem("row_sum_inv_done")
        s_Pn = [sem("prob_low_normed"), sem("prob_high_normed")]
        s_T = sem("prob_transposed")
        s_E = [sem("pt_even_done"), sem("pt_odd_done")]
        s_O = sem("attn_product")
        s_Oy = sem("y_attn_done")

        def tile_of(n):
            return n // NT % 2, ORDER[n % NT]

        def prob(n):
            return (prs if n % 2 else prb)[n // 2 % 2]

        def logits_at(n):
            return psum[4] if n % 2 else psum2[n // 2 % 2]

        def banks_until(n):
            return 3 * (n // 2) + (3 if n % 2 else 2)

        def banks(n):
            first, tiles = 3 * (n // 2) + 2 * (n % 2), tile_of(n)[1] + 1
            return [(first + b, 4 * b, min(4, tiles - 4 * b)) for b in range(1 if n % 2 else 2)]

        def product_number(h2, g):
            return 4 * h2 + list(PRODUCT_AT.values()).index(g)

        with nc.Block() as block:
            @block.sync
            def _(sp):
                def load_head(h, s):
                    q = bass.ds(h * HD, HD)
                    sp.dma_start(QC[s][0:HD], qk_d[0, q]).then_inc(s_ld[s], 16)
                    sp.dma_start(KC[s][0:HD], qk_d[1, q]).then_inc(s_ld[s], 16)
                    sp.dma_start(KC[s][HD:HD + 1], negc_d[bass.ds(h, 1), :]).then_inc(s_ld[s], 16)
                    sp.dma_start(VH[s][:], v_d[:, q].rearrange("(k p) d -> p k d", p=P)).then_inc(s_ld[s], 16)

                for slot in range(2):
                    sp.wait_ge(s_st[slot], 16 * 5)
                load_head(0, 0)
                load_head(1, 1)
                sp.dma_start(ypool[:], yp_d.rearrange("(g p) t -> p g t", p=P)).then_inc(s_mc, 16)
                sp.dma_start(gfr[:], g_ffn.to_broadcast([P, D])).then_inc(s_mc, 16)
                for slot in range(4):
                    sp.wait_ge(s_st[slot], 16 * 6)
                for c in range(4):
                    sp.dma_start(raw[c][:], item_chunk(0, c)).then_inc(s_raw[c], 16)
                with sp.Fori(0, NH // 2 - 1) as j:
                    for s in range(2):
                        sp.wait_ge(s_O, NPROD * j + NPROD + 4 * (s + 1))
                        load_head(2 * j + 2 + s, s)

            @block.gpsimd
            def _(pool):
                with pool.Fori(0, NH // 2) as j:
                    for n in range(QT):
                        w = min(tile_of(n)[1] + 1, 4) * P
                        pool.wait_ge(s_rr, QT * j + n + 1)
                        pool.tensor_tensor(prob(n)[:, 0:w], prob(n)[:, 0:w], rrs[:, n:n + 1].to_broadcast([P, w]),
                                           ALU.mult).then_inc(s_Pn[0], 1)

            def evac_pt(eng, j, n, parity):
                h2, qi = tile_of(n)
                for tb, k0, blocks in banks(n):
                    if tb % 2 != parity:
                        continue
                    eng.wait_ge(s_T, TB * j + 6 + tb + 1)
                    eng.wait_ge(s_O, NPROD * j + product_number(h2, qi // 2) + 1)
                    dst = pt[h2][qi // 2][:, k0:k0 + blocks, (qi % 2) * P:(qi % 2 + 1) * P]
                    src = psum[5 + parity][:, 0:blocks * P].rearrange("p (k t) -> p k t", t=P)
                    if parity == 0:
                        eng.activation(dst, src, ACT.Copy).then_inc(s_E[0], 1)
                    else:
                        eng.tensor_copy(dst, src).then_inc(s_E[1], 1)

            @block.scalar
            def _(act):
                act.sem_inc(s_P, 4)
                act.sem_inc(s_E[0], 1)
                act.sem_inc(s_Oy, 1)

                def exp(j, n):
                    w, c = (tile_of(n)[1] + 1) * P, n % QT
                    act.wait_ge(s_nm, QT * j + n + 1)
                    act.wait_ge(s_T, TB * j + 6 + banks_until(n - 4))
                    act.activation(prob(n)[:, 0:w], logits_at(n)[:, 0:w], ACT.Exp, bias=nmx[:, c:c + 1],
                                   accum_out=rsm[:, c:c + 1]).then_inc(s_P, 1)

                def y_out(j, h2, g):
                    o = product_number(h2, g)
                    act.wait_ge(s_O, NPROD * j + NPROD + o + 1)
                    r = HD * h2
                    act.activation(ya[r:r + HD, bass.ds(j, 1), g * 2 * P:(g + 1) * 2 * P],
                                   psum[7][0:HD, 0:2 * P].unsqueeze(1), ACT.Copy).then_inc(s_Oy, 1)

                exp(0, 0)
                with act.Fori(0, NH // 2) as j:
                    for n in range(QT):
                        if n + 1 < QT:
                            exp(j, n + 1)
                        else:
                            with act.If(j + 1 < NH // 2):
                                exp(j, QT)
                        evac_pt(act, j, n, 0)
                        for h2 in range(2):
                            if n - NT * h2 in PRODUCT_AT:
                                y_out(j, h2, PRODUCT_AT[n - NT * h2])
                    for g in (2, 1):
                        y_out(j, 1, g)

            @block.vector
            def _(dve):
                dve.sem_inc(s_E[1], 1)

                def neg_max(j, n):
                    w, c = (tile_of(n)[1] + 1) * P, n % QT
                    dve.wait_ge(s_S, QT * j + n + 1)
                    dve.tensor_reduce(nmx[:, c:c + 1], logits_at(n)[:, 0:w], AX.X, ALU.max,
                                      negate=True).then_inc(s_nm, 1)

                def norm(j, n):
                    w, c = (tile_of(n)[1] + 1) * P, n % QT
                    dve.wait_ge(s_P, QT * j + n + 5)
                    dve.reciprocal(rrs[:, c:c + 1], rsm[:, c:c + 1]).then_inc(s_rr, 1)
                    if n % 2 == 0:
                        dve.wait_ge(s_rr, QT * j + n + 1)
                        dve.tensor_scalar(prob(n)[:, 512:w], prob(n)[:, 512:w], rrs[:, c:c + 1], None,
                                          ALU.mult).then_inc(s_Pn[1], 1)

                neg_max(0, 0)
                neg_max(0, 1)
                norm(0, 0)
                with dve.Fori(0, NH // 2) as j:
                    for n in range(QT):
                        if n + 2 < QT:
                            norm(j, n + 1)
                            neg_max(j, n + 2)
                        elif n + 2 == QT:
                            norm(j, n + 1)
                            with dve.If(j + 1 < NH // 2):
                                neg_max(j, QT)
                        else:
                            with dve.If(j + 1 < NH // 2):
                                norm(j, QT)
                                neg_max(j, QT + 1)
                        evac_pt(dve, j, n, 1)

            @block.tensor
            def _(pe):
                pe.sem_inc(s_T, 6)
                pe.sem_inc(s_O, NPROD)
                pe.wait_ge(s_on, 8)

                def logits(j, n):
                    h2, qi = tile_of(n)
                    if n % NT == 0:
                        pe.wait_ge(s_ld[h2], 64 * j + 64 * (n // QT + 1))
                    pe.wait_ge(s_P, QT * j + n + (3 if n % 2 else 1))
                    w, o = (qi + 1) * P, logits_at(n)
                    for c0 in range(0, w, 512):
                        c1 = min(c0 + 512, w)
                        pe.matmul(o[:, c0:c1], QC[h2][:, qi * P:(qi + 1) * P], KC[h2][:, c0:c1],
                                  start=True, stop=c1 < w)
                    pe.matmul(o[:, w - P:w], identb[:], maskb[:], start=False, stop=True).then_inc(s_S, 1)

                def transposes(j, n):
                    for tb, k0, blocks in banks(n):
                        pe.wait_ge(s_E[tb % 2], TB // 2 * j + tb // 2 + 1)
                        if k0 == 0:
                            pe.wait_ge(s_Pn[0], QT * j + n + 1)
                        else:
                            pe.wait_ge(s_Pn[1], NT * j + n // 2 + 1)
                        for b in range(blocks):
                            last = pe.transpose(psum[5 + tb % 2][:, b * P:(b + 1) * P],
                                                prob(n)[:, (k0 + b) * P:(k0 + b + 1) * P], ident[:])
                        last.then_inc(s_T, 1)

                def product(j, h2, g):
                    last_step = NT * h2 + max(ORDER.index(2 * g), ORDER.index(2 * g + 1))
                    for e in range(2):
                        pe.wait_ge(s_E[e], TB // 2 * j + 1 + (banks_until(last_step) + 1 - e) // 2)
                    pe.wait_ge(s_Oy, NPROD * j + product_number(h2, g) + 1)
                    last_k = 2 * g + 1
                    for k in range(last_k + 1):
                        c = P if k == last_k else 0
                        last = pe.matmul(psum[7][0:HD, c:2 * P], VH[h2][:, k, :], pt[h2][g][:, k, c:2 * P],
                                         start=(k == 0), stop=(k == last_k))
                    last.then_inc(s_O, 1)

                logits(0, 0)
                logits(0, 1)
                with pe.Fori(0, NH // 2) as j:
                    for n in range(QT):
                        if n + 2 < QT:
                            logits(j, n + 2)
                        else:
                            with pe.If(j + 1 < NH // 2):
                                logits(j, n + 2)
                        transposes(j, n)
                        for h2 in range(2):
                            if n - NT * h2 in PRODUCT_AT:
                                product(j, h2, PRODUCT_AT[n - NT * h2])
                    for g in (2, 1):
                        product(j, 1, g)

        if phases < 3:
            return

        m = Map(nc, mix_at, mix_end)
        late_at = end - 2 * (NT * NE + SLOTS + 2 * NT)
        m2 = Map(nc, late_at, end)
        msk = m2.take("chosen", [P, NT, NE], BF16)
        ios = m2.take("iota_slot", [P, SLOTS], BF16)
        tok2 = m2.take("token_id", [P, NT, 2], BF16)
        m2 = Map(nc, mix_end + 4 * (4 * S + D), late_at)
        tri = m2.take("tri", [P, P], BF16)
        onb = m2.take("ones_b", [P, P], BF16)
        trif = m2.take("tri_f", [P, P], F32)
        onf = m2.take("ones_ff", [P, P], F32)
        ioi = m2.take("iota_item", [P, ITEMS], F32)
        bul = m2.take("b_up_rows", [NE, 2 * D], F32)
        s_dc = sem("disp_consts")
        s_dl = sem("disp_landed")
        BIGI = 4096
        xr = [m.take(f"x_res{i}", [P, D], F32) for i in range(2)]
        x2 = [m.take(f"x2_{i}", [P, D], F32) for i in range(4)]
        h2r = [m.take(f"h2_row{i}", [P, ROW], F32) for i in range(4)]
        h2t = m.take("h2_t", [P, KT, P], F32)
        wr = m.take("w_router_sb", [P, KT, NE], F32)
        brr = m.take("b_router_row", [P, NE], F32)
        lg = m.take("router_logits", [P, NE], F32)
        top8 = m.take("top8", [P, 8], F32)
        ix8 = m.take("index8", [P, 8], U32)
        ixf = m.take("index_f", [P, TOPK], F32)
        ex = m.take("gate_exp", [P, TOPK], F32)
        tiny = m.take("tiny", [P, 8], F32)
        gat = m.take("gates", [P, TOPK], F32)
        ohe = m.take("one_hot", [P, TOPK, NE], F32)
        ohg = m.take("one_hot_gate", [P, TOPK, NE], F32)
        bdn = m.take("b_down_sb", [NE, D], F32)
        gtt = m.take("gates_t", [NE, P], F32)
        ioe = m.take("iota_e", [P, NE], F32)

        s_io = sem("iota_e_set")
        s_xr = [sem(f"x_res_landed{i}") for i in range(2)]
        s_og = sem("out_proj_done")
        s_x2 = sem("x2_done")
        s_xs = sem("x2_squares")
        s_xi = sem("x2_rstd")
        s_ex = sem("gate_exp_done")
        s_rv = sem("router_dve")
        s_h2 = sem("h2_done")
        s_tt = sem("h2_transposed")
        s_te = sem("h2_t_done")
        s_rl = sem("router_product")
        s_gt = sem("gates_transposed")
        s_gd = sem("gates_t_done")
        s_bd = sem("bias_product")
        s_ac = sem("acc_done")
        s_hs = [sem(f"h2_stored{i}") for i in range(4)]
        s_as = [sem(f"acc_stored{i}") for i in range(4)]
        RV = 11

        with nc.Block() as block:
            @block.sync
            def _(sp):
                for i in range(NT):
                    if i >= 2:
                        sp.wait_ge(s_x2, 2 * (i - 1))
                    sp.dma_start(xr[i % 2][:], x_rows[i * P:(i + 1) * P, :]).then_inc(s_xr[i % 2], 16)
                    if i == 1:
                        sp.dma_start(wr[:], w_router[0].rearrange("(k p) e -> p k e", p=P)).then_inc(s_mc, 16)
                        sp.dma_start(brr[:], b_router.to_broadcast([P, NE])).then_inc(s_mc, 16)
                        sp.dma_start(bdn[:], b_down[0]).then_inc(s_mc, 16)
                        sp.dma_start(bul[:], b_up[0]).then_inc(s_dl, 16)
                for c in range(4, NCH):
                    sp.wait_ge(s_og, 2 * NT)
                    sp.dma_start(raw[c][:], item_chunk(0, c)).then_inc(s_raw[c], 16)

            @block.gpsimd
            def _(pool):
                pool.iota(ioe[:], pattern=[[1, NE]], base=0, channel_multiplier=0,
                          allow_small_or_imprecise_dtypes=True).then_inc(s_io, 1)
                pool.memset(onf[:], 1.0).then_inc(s_dc, 1)
                pool.memset(onb[:], 1.0).then_inc(s_dc, 1)
                pool.wait_ge(s_dc, 2)
                pool.affine_select(out=tri[:], in_=onb[:], pattern=[[1, P]], compare_op=ALU.is_gt, fill=0.0,
                                   base=0, channel_multiplier=-1).then_inc(s_dc, 1)
                pool.affine_select(out=trif[:], in_=onf[:], pattern=[[1, P]], compare_op=ALU.is_gt, fill=0.0,
                                   base=0, channel_multiplier=-1).then_inc(s_dc, 1)
                pool.iota(ioi[:], pattern=[[1, ITEMS]], base=0, channel_multiplier=0,
                          allow_small_or_imprecise_dtypes=True).then_inc(s_dc, 1)
                pool.iota(ios[:], pattern=[[1, SLOTS]], base=0, channel_multiplier=0,
                          allow_small_or_imprecise_dtypes=True).then_inc(s_dc, 1)
                pool.iota(tok2[:, :, 0:1], pattern=[[0, NT]], base=0, channel_multiplier=1,
                          allow_small_or_imprecise_dtypes=True).then_inc(s_dc, 1)
                pool.iota(tok2[:, :, 1:2], pattern=[[P, NT]], base=-BIGI, channel_multiplier=0,
                          allow_small_or_imprecise_dtypes=True).then_inc(s_dc, 1)
                for i in range(NT + 2):
                    if i >= 2:
                        t = i - 2
                        pool.wait_ge(s_ac, 2 * t + 2)
                        pool.dma_start(acc_d[t * P:(t + 1) * P, :], x2[t % 4][:]).then_inc(s_as[t % 4], 16)
                    if i < NT:
                        pool.wait_ge(s_rv, RV * i + RV)
                        pool.dma_start(h2g_d[i * P:(i + 1) * P, :], h2r[i % 4][:]).then_inc(s_hs[i % 4], 16)
                for s in range(4):
                    pool.wait_ge(s_hs[s], 16 * NT // 4)
                    pool.wait_ge(s_as[s], 16 * NT // 4)

            @block.scalar
            def _(act):
                def norm(i):
                    act.wait_ge(s_x2, 2 * i + 2)
                    if i >= 4:
                        act.wait_ge(s_hs[i % 4], 16 * (i // 4))
                    if i >= 1:
                        act.wait_ge(s_xi, i)
                    act.activation(h2r[i % 4][:, 0:D], x2[i % 4][:], ACT.Square, accum_out=tiny[:, 3:4]).then_inc(s_xs, 1)
                    act.wait_ge(s_xs, 2 * i + 1)
                    act.activation(tiny[:, 4:5], tiny[:, 3:4], ACT.Sqrt, bias=epsb[:], scale=1.0 / D).then_inc(s_xs, 1)

                def h2_t(i):
                    for b in range(2):
                        act.wait_ge(s_tt, 2 * i + b + 1)
                        act.activation(h2t[:, 4 * b:4 * b + 4, :], psum[4 + b][:].rearrange("p (k t) -> p k t", k=4),
                                       ACT.Copy).then_inc(s_te, 1)

                def gates(i):
                    act.wait_ge(s_rv, RV * i + 3)
                    act.activation(ex[:], top8[:, 0:TOPK], ACT.Exp, bias=tiny[:, 0:1], accum_out=tiny[:, 1:2]).then_inc(s_ex, 1)

                def gates_t(i):
                    act.wait_ge(s_gt, i + 1)
                    act.activation(gtt[:], psum[7][0:NE, 0:P], ACT.Copy).then_inc(s_gd, 1)

                for i in range(NT + 2):
                    if 1 <= i < NT + 1:
                        h2_t(i - 1)
                    if i >= 2:
                        gates_t(i - 2)
                    if i < NT:
                        norm(i)
                    if 1 <= i < NT + 1:
                        gates(i - 1)

            @block.vector
            def _(dve):
                dve.wait_ge(s_mc, 80)
                dve.wait_ge(s_io, 1)

                def residual(i, half):
                    c = slice(half * 512, (half + 1) * 512)
                    dve.wait_ge(s_og, 2 * i + half + 1)
                    dve.wait_ge(s_xr[i % 2], 16 * (i // 2 + 1))
                    if i >= 4:
                        dve.wait_ge(s_as[i % 4], 16 * (i // 4))
                    dve.tensor_tensor(x2[i % 4][:, c], psum[2 * (i % 2) + half][:], xr[i % 2][:, c], ALU.add).then_inc(s_x2, 1)

                def norm(i):
                    dve.wait_ge(s_xs, 2 * i + 2)
                    dve.reciprocal(tiny[:, 5:6], tiny[:, 4:5]).then_inc(s_xi, 1)
                    dve.wait_ge(s_xi, i + 1)
                    dve.scalar_tensor_tensor(out=h2r[i % 4][:, 0:D], in0=x2[i % 4][:], scalar=tiny[:, 5:6], in1=gfr[:],
                                             op0=ALU.mult, op1=ALU.mult).then_inc(s_h2, 1)

                def gates(i):
                    n = RV * i
                    dve.wait_ge(s_rl, i + 1)
                    dve.tensor_tensor(lg[:], psum[6][:, 0:NE], brr[:], ALU.add).then_inc(s_rv, 1)
                    dve.wait_ge(s_rv, n + 1)
                    dve.max(top8[:], lg[:]).then_inc(s_rv, 1)
                    dve.wait_ge(s_rv, n + 2)
                    dve.tensor_scalar(tiny[:, 0:1], top8[:, 0:1], -1.0, None, ALU.mult).then_inc(s_rv, 1)
                    dve.max_index(ix8[:], top8[:], lg[:]).then_inc(s_rv, 1)
                    dve.wait_ge(s_rv, n + 4)
                    dve.tensor_copy(ixf[:], ix8[:, 0:TOPK]).then_inc(s_rv, 1)
                    dve.wait_ge(s_rv, n + 5)
                    dve.tensor_tensor(ohe[:], ioe[:].unsqueeze(1).to_broadcast([P, TOPK, NE]),
                                      ixf[:].unsqueeze(2).to_broadcast([P, TOPK, NE]), ALU.is_equal).then_inc(s_rv, 1)
                    dve.wait_ge(s_ex, i + 1)
                    dve.reciprocal(tiny[:, 2:3], tiny[:, 1:2]).then_inc(s_rv, 1)
                    dve.wait_ge(s_rv, n + 7)
                    dve.tensor_scalar(gat[:], ex[:], tiny[:, 2:3], None, ALU.mult).then_inc(s_rv, 1)
                    dve.wait_ge(s_rv, n + 8)
                    dve.tensor_tensor(ohg[:], ohe[:], gat[:].unsqueeze(2).to_broadcast([P, TOPK, NE]), ALU.mult).then_inc(s_rv, 1)
                    with nc.allow_low_precision(reason="a sum of four values that are 0 or 1, one at most 1"):
                        dve.tensor_reduce(msk[:, i, :], ohe[:].rearrange("p j e -> p e j"), AX.X, ALU.add).then_inc(s_rv, 1)
                    dve.wait_ge(s_rv, n + 10)
                    dve.tensor_reduce(h2r[i % 4][:, D:ROW], ohg[:].rearrange("p j e -> p e j"), AX.X, ALU.add).then_inc(s_rv, 1)

                def acc(i, half):
                    c = slice(half * 512, (half + 1) * 512)
                    dve.wait_ge(s_bd, 2 * i + half + 1)
                    dve.tensor_tensor(x2[i % 4][:, c], psum[7][:], x2[i % 4][:, c], ALU.add).then_inc(s_ac, 1)

                for i in range(NT + 3):
                    if i < NT:
                        residual(i, 0)
                    if i >= 3:
                        acc(i - 3, 1)
                    if i < NT:
                        residual(i, 1)
                        norm(i)
                    if 1 <= i < NT + 1:
                        gates(i - 1)
                    if 2 <= i < NT + 2:
                        acc(i - 2, 0)

            @block.tensor
            def _(pe):
                pe.wait_ge(s_mc, 32)

                def out_proj(i, half):
                    tok = slice(i * P, (i + 1) * P)
                    if i == 0:
                        pe.wait_ge(s_raw[4 + half], 16)
                    if i >= 2:
                        pe.wait_ge(s_x2, 2 * (i - 2) + half + 1)
                    for k in range(KT):
                        y = ypool[:, k, tok] if k < 4 else ya[:, k - 4, tok]
                        last = pe.matmul(psum[2 * (i % 2) + half][:], y, raw[4 + half][:, k, :],
                                         start=(k == 0), stop=(k == KT - 1))
                    last.then_inc(s_og, 1)

                def h2_transposes(i):
                    pe.wait_ge(s_h2, i + 1)
                    for b in range(2):
                        if i >= 1:
                            pe.wait_ge(s_te, 2 * (i - 1) + b + 1)
                        for j in range(4):
                            k = 4 * b + j
                            last = pe.transpose(psum[4 + b][:, j * P:(j + 1) * P], h2r[i % 4][:, k * P:(k + 1) * P], ident[:])
                        last.then_inc(s_tt, 1)

                def route(i):
                    if i == 0:
                        pe.wait_ge(s_mc, 80)
                    pe.wait_ge(s_te, 2 * i + 2)
                    if i >= 1:
                        pe.wait_ge(s_rv, RV * (i - 1) + 1)
                    for k in range(KT):
                        last = pe.matmul(psum[6][:, 0:NE], h2t[:, k, :], wr[:, k, :], start=(k == 0), stop=(k == KT - 1))
                    last.then_inc(s_rl, 1)

                def gates_transpose(i):
                    pe.wait_ge(s_rv, RV * i + RV)
                    if i >= 1:
                        pe.wait_ge(s_ac, 2 * i)
                    pe.transpose(psum[7][0:NE, 0:P], h2r[i % 4][:, D:ROW], ident[:]).then_inc(s_gt, 1)

                def bias(i, half):
                    if half == 0:
                        pe.wait_ge(s_gd, i + 1)
                    else:
                        pe.wait_ge(s_ac, 2 * i + 1)
                    pe.matmul(psum[7][:], gtt[:], bdn[:, half * 512:(half + 1) * 512], start=True,
                              stop=True).then_inc(s_bd, 1)

                for i in range(NT + 3):
                    if i < NT:
                        out_proj(i, 0)
                    if i >= 3:
                        bias(i - 3, 1)
                    if 1 <= i < NT + 1:
                        h2_transposes(i - 1)
                    if 2 <= i < NT + 2:
                        gates_transpose(i - 2)
                    if i < NT:
                        out_proj(i, 1)
                    if 1 <= i < NT + 1:
                        route(i - 1)
                    if 2 <= i < NT + 2:
                        bias(i - 2, 0)

        if phases < 4:
            return

        m = phase()
        m.end = mix_end + 4 * (4 * S + D)
        posm = m.take("position", [P, NT, NE], F32)
        tab = m.take("item_table", [P, 3, ITEMS], I32)
        tbf = m.take("item_base", [P, ITEMS], F32)
        nit = m.take("item_count", [P, 1], I32)
        bup = m.take("b_up_t", [P, 2 * KT, NE], F32)
        moe_at = m.at
        sm = m.take("small", [NE, 16], F32)
        ab = m.take("item_masks", [NE, 3, ITEMS], F32)
        ttmp = m.take("table_tmp", [P, 3, ITEMS], F32)
        s_dp = sem("disp_pe")
        s_dv = sem("disp_dve")

        with nc.Block() as block:
            @block.tensor
            def _(pe):
                pe.wait_ge(s_dc, 8)
                for i in range(NT):
                    o = psum[0][:, i * NE:(i + 1) * NE]
                    for j in range(i):
                        pe.matmul(o, onb[:], msk[:, j, :], start=(j == 0), stop=False)
                    last = pe.matmul(o, tri[:], msk[:, i, :], start=(i == 0), stop=True)
                last.then_inc(s_dp, 1)
                for i in range(NT):
                    last = pe.matmul(psum[1][0:NE, 0:1], msk[:, i, :], onb[:, 0:1], start=(i == 0), stop=(i == NT - 1))
                last.then_inc(s_dp, 1)
                pe.wait_ge(s_dl, 16)
                for t in range(2 * KT):
                    last = pe.transpose(psum[2][:, t * NE:(t + 1) * NE], bul[:, t * P:(t + 1) * P], ident[0:NE, 0:NE])
                last.then_inc(s_dp, 1)
                pe.wait_ge(s_dv, 8)
                pe.matmul(psum[3][0:NE, 0:1], trif[0:NE, 0:NE], sm[:, 1:2], start=True, stop=True).then_inc(s_dp, 1)
                pe.wait_ge(s_dv, 15)
                pe.matmul(psum[4][:, 0:3 * ITEMS], onf[0:NE, :], ab[:].rearrange("e a i -> e (a i)"), start=True, stop=True)
                pe.matmul(psum[4][:, 256:257], onf[0:NE, :], sm[:, 1:2], start=True, stop=True).then_inc(s_dp, 1)

            @block.vector
            def _(dve):
                step = [0]

                def done(ins):
                    step[0] += 1
                    ins.then_inc(s_dv, 1)
                    dve.wait_ge(s_dv, step[0])

                dve.wait_ge(s_dc, 8)
                dve.wait_ge(s_dp, 1)
                mk = msk[:].rearrange("p i e -> p (i e)")
                pm = posm[:].rearrange("p i e -> p (i e)")
                done(dve.scalar_tensor_tensor(out=pm, in0=psum[0][:, 0:NT * NE], scalar=1.0, in1=mk,
                                              op0=ALU.add, op1=ALU.mult))
                done(dve.tensor_scalar(pm, pm, -1.0, None, ALU.add))
                dve.wait_ge(s_dp, 2)
                done(dve.tensor_copy(sm[:, 0:1], psum[1][0:NE, 0:1]))
                done(dve.tensor_scalar(sm[:, 1:2], sm[:, 0:1], SLOTS + 0.5, 1.0, ALU.is_gt, ALU.add))
                src = 1
                for q in range(2, 6):
                    dst = 3 - src
                    done(dve.scalar_tensor_tensor(out=sm[:, dst:dst + 1], in0=sm[:, 0:1], scalar=q * SLOTS + 0.5,
                                                  in1=sm[:, src:src + 1], op0=ALU.is_gt, op1=ALU.add))
                    src = dst
                assert src == 1 and step[0] == 8
                dve.wait_ge(s_dp, 4)
                done(dve.tensor_copy(sm[:, 3:4], psum[3][0:NE, 0:1]))
                done(dve.tensor_tensor(sm[:, 4:5], sm[:, 3:4], sm[:, 1:2], ALU.add))
                done(dve.tensor_scalar(ab[:, 0, :], ioi[0:NE, :], sm[:, 3:4], None, ALU.is_ge))
                done(dve.tensor_scalar(ab[:, 1, :], ioi[0:NE, :], sm[:, 4:5], None, ALU.is_ge))
                done(dve.tensor_tensor(ab[:, 2, :], ab[:, 0, :], ab[:, 1, :], ALU.subtract))
                done(dve.tensor_scalar(ab[:, 2, :], ab[:, 2, :], sm[:, 0:1], None, ALU.mult))
                done(dve.tensor_scalar(ab[:, 1, :], ab[:, 1, :], sm[:, 1:2], None, ALU.mult))
                dve.wait_ge(s_dp, 5)
                done(dve.tensor_copy(ttmp[:], psum[4][:, 0:3 * ITEMS].rearrange("p (a i) -> p a i", a=3)))
                done(dve.tensor_copy(nit[:], psum[4][:, 256:257]))
                done(dve.tensor_scalar(tab[:, 0, :], ttmp[:, 0, :], -1.0, 0.0, ALU.add, ALU.max))
                done(dve.tensor_tensor(tbf[:], ioi[:], ttmp[:, 1, :], ALU.subtract))
                done(dve.tensor_scalar(tbf[:], tbf[:], float(SLOTS), None, ALU.mult))
                done(dve.tensor_tensor(tab[:, 1, :], ttmp[:, 2, :], tbf[:], ALU.subtract))
                dve.wait_ge(s_dp, 3)
                done(dve.tensor_copy(bup[:, 0:KT, :], psum[2][:, 0:KT * NE].rearrange("p (t e) -> p t e", t=KT)))
                done(dve.tensor_scalar(bup[:, KT:, :], psum[2][:, KT * NE:].rearrange("p (t e) -> p t e", t=KT),
                                       1.0, None, ALU.add))
        if phases < 5:
            return

        m = phase()
        m.at, m.end = moe_at, late_at
        xg = m.take("xg", [P, KT, SLOTS], F32)
        rows = [m.take(f"xg_rows{b}", [P, ROW], F32) for b in range(2)]
        gl = m.take("glu", [P, 4, SLOTS], F32)
        sg = m.take("glu_sigmoid", [P, 4, SLOTS], F32)
        ln_ = m.take("lin", [P, 4, SLOTS], F32)
        tm = m.take("glu_lin", [P, 4, SLOTS], F32)
        hid = m.take("hidden", [P, KT, SLOTS], F32)
        yt = m.take("y_t", [P, KT, SLOTS], F32)
        wlo = [m.take(f"w_down_rest{i}", [P, KT, CW], F32R) for i in range(2)]
        uh = m.take("hidden_r", [P, KT, P], F32R)
        ul = m.take("hidden_rest", [P, KT, P], F32R)
        yr = [m.take(f"y_rows{b}", [P, D], F32) for b in range(2)]
        sel = m.take("select", [P, NT, 2 * P], BF16)
        pcol = m.take("position_col", [P, NT], F32)
        ixs = m.take("row_index_sum", [P, 2], F32)
        ixn = m.take("row_index_next", [P, 2], U32)
        ixc = m.take("row_index_now", [P, 2], U32)
        gn = m.take("gate_next", [P, 2], F32)
        gc = m.take("gate_now", [P, 2], F32)
        BLK = (P, SLOTS - P)

        s_z = sem("moe_zeroed")
        s_pc = sem("position_col_done")
        s_sel = sem("select_done")
        s_ip = sem("index_product")
        s_is = sem("index_sum_done")
        s_ix = sem("index_done")
        s_rw = sem("rows_landed")
        s_xt = sem("x_transposed")
        s_xe = [sem("xg_even_done"), sem("xg_odd_done")]
        s_gn = sem("gate_next_done")
        s_cur = sem("index_gate_now")
        s_evd = sem("up_evacuated")
        s_eva = sem("down_evacuated")
        s_sg = sem("sigmoid_done")
        s_tm = sem("glu_lin_done")
        s_hf = sem("hidden_done")
        s_wa = sem("w_down_rounded")
        s_wb = sem("w_down_rest_done")
        s_wc = sem("w_down_split")
        s_uh = sem("hidden_r_done")
        s_ul = sem("hidden_rest_done")
        s_yt = sem("y_transposed")
        s_ye = sem("y_rows_done")
        s_sc = sem("scatter_landed")
        s_sd = sem("scatters_done")

        GLU = (0, 2)

        with nc.Block() as block:
            def split_width(eng, n, f):
                def pick(widths):
                    if len(widths) == 1:
                        f(widths[0])
                        return
                    with eng.If(n < widths[0] + 1):
                        f(widths[0])
                    with eng.Else():
                        pick(widths[1:])

                pick(WIDTHS)

            @block.sync
            def _(sp):
                n_items = sp.value_load(nit[0:1, 0:1], min_val=NE, max_val=MAX_ITEMS)
                with sp.Fori(0, n_items - 1) as i:
                    e = sp.value_load(tab[0:1, 0, bass.ds(i + 1, 1)], min_val=0, max_val=NE - 1)
                    for c in range(NCH):
                        sp.wait_ge(s_pd, i * NCH + (c + 1))
                        sp.dma_start(raw[c][:], item_chunk(e, c)).then_inc(s_raw[c], 16)

            @block.gpsimd
            def _(pool):
                for b in range(2):
                    pool.memset(rows[b][:], 0.0).then_inc(s_z, 1)
                pool.memset(sel[:, :, SLOTS:], 0.0).then_inc(s_z, 1)
                pool.memset(yt[:], 0.0).then_inc(s_z, 1)
                pool.memset(yr[1][:], 0.0).then_inc(s_z, 1)
                n_items = pool.value_load(nit[0:1, 0:1], min_val=NE, max_val=MAX_ITEMS)

                rows_less_2, last_row = pool.alloc_register("rows_less_2"), pool.alloc_register("last_row")
                pool.reg_mov(rows_less_2, S - 2)

                def gather(i):
                    pool.wait_ge(s_ix, i + 1)
                    pool.reg_add(last_row, rows_less_2, 1)
                    for b in range(2):
                        pool.indirect_dma_start(out=rows[b][0:BLK[b], :], out_offset=None, in_=h2g_d,
                                                in_offset=bass.IndirectOffsetOnAxis(ap=ixn[0:BLK[b], b:b + 1], axis=0),
                                                bounds_check=last_row, oob_is_err=False).then_inc(s_rw, 16)

                pool.sem_inc(s_sd, 1)
                pool.wait_ge(s_z, 6)
                gather(0)
                with pool.Fori(0, n_items) as i:
                    with pool.If(i + 1 < n_items):
                        gather(i + 1)
                    pool.wait_ge(s_ye, 4 * i + 5)
                    pool.wait_ge(s_eva, 2 * i + 4)
                    pool.reg_add(last_row, rows_less_2, 1)
                    for b in range(2):
                        pool.indirect_dma_start(out=acc_d, out_offset=bass.IndirectOffsetOnAxis(ap=ixc[0:BLK[b], b:b + 1], axis=0),
                                                in_=yr[b][0:BLK[b], :], in_offset=None, bounds_check=last_row,
                                                oob_is_err=False, compute_op=ALU.add).then_inc(s_sc, 16)
                    pool.wait_ge(s_sc, i * 32 + 32)
                    pool.sem_inc(s_sd, 1)

            def quarter(t, q):
                return t[:, 2 * q:2 * q + 2, :]

            def x_evac(eng, i, parity):
                for r in range(parity, 4, 2):
                    eng.wait_ge(s_xt, 4 * i + r + 1)
                    dst = xg[:, 2 * r:2 * r + 2, :]
                    src = psum[4 + r][:, 0:2 * SLOTS].rearrange("p (k t) -> p k t", k=2)
                    if parity == 0:
                        eng.activation(dst, src, ACT.Copy).then_inc(s_xe[0], 1)
                    else:
                        eng.tensor_copy(dst, src).then_inc(s_xe[1], 1)

            @block.scalar
            def _(act):
                act.sem_inc(s_eva, 2)
                act.sem_inc(s_ye, 1)
                n_items = act.value_load(nit[0:1, 0:1], min_val=NE, max_val=MAX_ITEMS)

                def round_copy(i, c):
                    act.wait_ge(s_raw[c], 16 * i + 32)
                    for q in range(4):
                        act.activation(quarter(wlo[c - 4], q), quarter(raw[c], q), ACT.Copy).then_inc(s_wa, 1)

                def round_chunk(i, c):
                    for q in range(4):
                        act.wait_ge(s_wb, 8 * i + 4 * (c - 4) + q + 1)
                        act.activation(quarter(raw_r[c], q), quarter(raw[c], q), ACT.Copy).then_inc(s_wc, 1)

                def round_hidden(i, part):
                    act.wait_ge(s_hf, 2 * i + part + 2)
                    act.activation(uh[:, 4 * part:4 * part + 4, :], hid[:, 4 * part:4 * part + 4, 0:P], ACT.Copy).then_inc(s_uh, 1)

                def sigmoids(i, w):
                    for part, c in enumerate(GLU):
                        act.wait_ge(s_evd, 4 * i + c + 1)
                        act.activation(sg[:, :, 0:w], gl[:, :, 0:w], ACT.Sigmoid, scale=ALPHA).then_inc(s_sg, 1)
                        if w == P:
                            round_copy(i, 4 + part)
                            if part == 0:
                                round_hidden(i, 0)
                            round_chunk(i, 4 + part)
                            if part == 1:
                                round_hidden(i, 1)
                    if w > P:
                        act.sem_inc(s_wa, 8)
                        act.sem_inc(s_wc, 8)
                        act.sem_inc(s_uh, 2)

                def y_evac(i, w):
                    if w == P:
                        act.wait_ge(s_sd, i + 1)
                        act.wait_ge(s_cur, i + 2)
                        for c in (4, 5):
                            act.wait_ge(s_pd, i * NCH + (c + 1))
                            for q in range(2):
                                last = act.activation(yr[0][:, (c - 4) * 512 + q * 256:(c - 4) * 512 + q * 256 + 256],
                                                      psum[2 * (c % 2)][:, q * 256:q * 256 + 256], ACT.Copy, scale=gc[:, 0:1])
                                if q == 0:
                                    last.then_inc(s_ye, 2)
                            last.then_inc(s_eva, 1)
                        return
                    for c in (4, 5):
                        act.wait_ge(s_pd, i * NCH + (c + 1))
                        if c == 4:
                            act.wait_ge(s_yt, 4 * i + 1)
                        for b in range(2):
                            last = act.activation(yt[:, 4 * (c - 4) + 2 * b:4 * (c - 4) + 2 * b + 2, 0:w],
                                                  psum[2 * (c % 2) + b][:, 0:2 * w].rearrange("p (k t) -> p k t", k=2),
                                                  ACT.Copy)
                        last.then_inc(s_eva, 1)
                    for half in range(2):
                        for b in range(2):
                            act.wait_ge(s_yt, 4 * i + 2 * half + b + 2)
                            if half == 0 and b == 0:
                                act.wait_ge(s_sd, i + 1)
                                act.wait_ge(s_cur, i + 2)
                            act.activation(yr[b][0:BLK[b], half * 512:(half + 1) * 512],
                                           psum[4 + 2 * half + b][0:BLK[b], :], ACT.Copy,
                                           scale=gc[0:BLK[b], b:b + 1]).then_inc(s_ye, 1)

                def by_width(i, f):
                    n = act.value_load(tab[0:1, 1, bass.ds(i, 1)], min_val=0, max_val=S)
                    split_width(act, n, f)

                act.wait_ge(s_z, 6)
                x_evac(act, 0, 0)
                with act.Fori(0, n_items) as i:
                    by_width(i, lambda w: sigmoids(i, w))
                    with act.If(i + 1 < n_items):
                        x_evac(act, i + 1, 0)
                    by_width(i, lambda w: y_evac(i, w))

            @block.vector
            def _(dve):
                n_items = dve.value_load(nit[0:1, 0:1], min_val=NE, max_val=MAX_ITEMS)
                dve.sem_inc(s_cur, 1)
                dve.sem_inc(s_hf, 1)
                dve.memset(gn[:], 0.0).then_inc(s_z, 1)

                def position_col(i):
                    e = dve.value_load(tab[0:1, 0, bass.ds(i, 1)], min_val=0, max_val=NE - 1)
                    dve.wait_ge(s_ip, i + 1)
                    dve.tensor_scalar(pcol[:].unsqueeze(2), posm[:, :, bass.ds(e, 1)], tbf[:, bass.ds(i, 1)], None,
                                      ALU.subtract).then_inc(s_pc, 1)
                    dve.wait_ge(s_pc, i + 1)
                    for t in range(NT):
                        last = dve.tensor_scalar(sel[:, t, 0:SLOTS], ios[:], pcol[:, t:t + 1], None, ALU.is_equal)
                    last.then_inc(s_sel, 1)

                def index(i):
                    dve.wait_ge(s_ip, i + 2)
                    dve.tensor_scalar(ixs[:], psum[4][:, 0:4].rearrange("p (b a) -> p b a", a=2)[:, :, 0], float(BIGI), None,
                                      ALU.add).then_inc(s_is, 1)
                    dve.wait_ge(s_is, i + 1)
                    dve.tensor_tensor(ixn[:], ixs[:], psum[4][:, 0:4].rearrange("p (b a) -> p b a", a=2)[:, :, 1],
                                      ALU.add).then_inc(s_ix, 1)

                def x_in(i):
                    e = dve.value_load(tab[0:1, 0, bass.ds(i, 1)], min_val=0, max_val=NE - 1)
                    dve.wait_ge(s_rw, 32 * i + 32)
                    dve.wait_ge(s_cur, i + 1)
                    for b in range(2):
                        dve.tensor_copy(gn[0:BLK[b], b:b + 1], rows[b][0:BLK[b], bass.ds(e + D, 1)]).then_inc(s_gn, 1)
                    x_evac(dve, i, 1)

                def weight_rest(i, c):
                    for q in range(4):
                        dve.wait_ge(s_wa, 8 * i + 4 * (c - 4) + q + 1)
                        dve.tensor_tensor(quarter(wlo[c - 4], q), quarter(raw[c], q), quarter(wlo[c - 4], q).bitcast(F32),
                                          ALU.subtract).then_inc(s_wb, 1)

                def hidden_rest(i, part):
                    dve.wait_ge(s_uh, 2 * i + part + 1)
                    h = slice(4 * part, 4 * part + 4)
                    dve.tensor_tensor(ul[:, h, :], hid[:, h, 0:P], uh[:, h, :].bitcast(F32), ALU.subtract).then_inc(s_ul, 1)

                def evac(i, w, c, e):
                    dve.wait_ge(s_pd, i * NCH + (c + 1))
                    part = c // 2
                    if c in GLU:
                        dve.wait_ge(s_hf, 2 * i + part + 1)
                        for t in range(4):
                            last = dve.tensor_scalar(gl[:, t, 0:w], psum[2 * (c % 2) + t // 2][:, (t % 2) * w:(t % 2 + 1) * w],
                                                     bup[:, 4 * part + t, bass.ds(e, 1)], LIMIT, ALU.add, ALU.min)
                        last.then_inc(s_evd, 1)
                        return
                    for t in range(4):
                        last = dve.tensor_scalar(ln_[:, t, 0:w], psum[2 * (c % 2) + t // 2][:, (t % 2) * w:(t % 2 + 1) * w],
                                                 bup[:, KT + 4 * part + t, bass.ds(e, 1)], LIMIT + 1.0, ALU.add, ALU.min)
                    last.then_inc(s_evd, 1)
                    dve.wait_ge(s_evd, 4 * i + c + 1)
                    dve.scalar_tensor_tensor(out=tm[:, :, 0:w], in0=ln_[:, :, 0:w], scalar=1.0 - LIMIT, in1=gl[:, :, 0:w],
                                             op0=ALU.max, op1=ALU.mult).then_inc(s_tm, 1)
                    dve.wait_ge(s_tm, 2 * i + part + 1)
                    dve.wait_ge(s_sg, 2 * i + part + 1)
                    dve.tensor_tensor(hid[:, 4 * part:4 * part + 4, 0:w], tm[:, :, 0:w], sg[:, :, 0:w],
                                      ALU.mult).then_inc(s_hf, 1)

                dve.wait_ge(s_z, 6)
                position_col(0)
                index(0)
                x_in(0)
                with dve.Fori(0, n_items) as i:
                    e = dve.value_load(tab[0:1, 0, bass.ds(i, 1)], min_val=0, max_val=NE - 1)
                    n = dve.value_load(tab[0:1, 1, bass.ds(i, 1)], min_val=0, max_val=S)
                    with dve.If(i + 1 < n_items):
                        position_col(i + 1)
                    split_width(dve, n, lambda w: evac(i, w, 0, e))
                    dve.wait_ge(s_sd, i + 1)
                    dve.wait_ge(s_ye, 4 * i + 1)
                    dve.wait_ge(s_eva, 2 * i + 2)
                    dve.wait_ge(s_gn, 2 * i + 2)
                    dve.wait_ge(s_ix, i + 1)
                    dve.tensor_copy(ixc[:], ixn[:])
                    dve.tensor_copy(gc[:], gn[:]).then_inc(s_cur, 1)
                    with dve.If(i + 1 < n_items):
                        index(i + 1)

                    def rest(w):
                        for c in range(1, 4):
                            evac(i, w, c, e)
                            if w == P:
                                if c == 1:
                                    weight_rest(i, 4)
                                    hidden_rest(i, 0)
                                elif c == 2:
                                    weight_rest(i, 5)
                                else:
                                    hidden_rest(i, 1)
                        if w > P:
                            dve.sem_inc(s_wb, 8)
                            dve.sem_inc(s_ul, 2)

                    split_width(dve, n, rest)
                    with dve.If(i + 1 < n_items):
                        x_in(i + 1)

            @block.tensor
            def _(pe):
                n_items = pe.value_load(nit[0:1, 0:1], min_val=NE, max_val=MAX_ITEMS)

                def index_product(i):
                    pe.wait_ge(s_sel, i + 1)
                    for b in range(2):
                        for t in range(NT):
                            last = pe.matmul(psum[4][:, 2 * b:2 * b + 2], sel[:, t, b * P:(b + 1) * P], tok2[:, t, :],
                                             start=(t == 0), stop=(t == NT - 1))
                    last.then_inc(s_ip, 1)

                def x_transposes(i):
                    pe.wait_ge(s_rw, 32 * i + 32)
                    pe.wait_ge(s_ix, i + 1)
                    for r in range(4):
                        for j in range(2):
                            k = 2 * r + j
                            pe.transpose(psum[4 + r][:, j * SLOTS:j * SLOTS + P], rows[0][:, k * P:(k + 1) * P], ident[:])
                            last = pe.transpose(psum[4 + r][:, j * SLOTS + P:(j + 1) * SLOTS],
                                                rows[1][0:BLK[1], k * P:(k + 1) * P], ident[0:BLK[1], 0:BLK[1]])
                        last.then_inc(s_xt, 1)

                def group(i, w, c):
                    if c == 0:
                        pe.wait_ge(s_eva, 2 * i + 1)
                        pe.wait_ge(s_xe[0], 2 * i + 2)
                        pe.wait_ge(s_xe[1], 2 * i + 2)
                    elif c == 1:
                        pe.wait_ge(s_eva, 2 * i + 2)
                    else:
                        pe.wait_ge(s_evd, 4 * i + c - 1)
                    pe.wait_ge(s_raw[c], 16 * i + 32)
                    src = xg if c < 4 else hid
                    if c >= 4 and w == P:
                        o, lo = psum[2 * (c % 2)][:], wlo[c - 4]
                        for k in range(KT):
                            if c == 4 and k % 4 == 0:
                                pe.wait_ge(s_ul, 2 * i + k // 4 + 1)
                            if k % 2 == 0:
                                pe.wait_ge(s_wc, 8 * i + 4 * (c - 4) + k // 2 + 1)
                            hi = raw_r[c][:, k, :]
                            pe.matmul(o, uh[:, k, :], hi, start=(k == 0), stop=False)
                            pe.matmul(o, uh[:, k, :], lo[:, k, :], start=False, stop=False)
                            last = pe.matmul(o, ul[:, k, :], hi, start=False, stop=(k == KT - 1))
                        last.then_inc(s_pd, 1)
                        return
                    for t in range(4):
                        o = psum[2 * (c % 2) + t // 2][:, (t % 2) * w:(t % 2 + 1) * w]
                        for k in range(KT):
                            if c == 4 and t == 0 and k % 4 == 0:
                                pe.wait_ge(s_hf, 2 * i + k // 4 + 2)
                            last = pe.matmul(o, raw[c][:, k, t * P:(t + 1) * P], src[:, k, 0:w],
                                             start=(k == 0), stop=(k == KT - 1))
                    last.then_inc(s_pd, 1)

                pe.sem_inc(s_ip, 1)
                pe.sem_inc(s_yt, 1)
                pe.wait_ge(s_z, 6)
                index_product(0)
                x_transposes(0)
                with pe.Fori(0, n_items) as i:
                    n = pe.value_load(tab[0:1, 1, bass.ds(i, 1)], min_val=0, max_val=S)

                    def up(cs):
                        def f(w):
                            for c in cs:
                                group(i, w, c)
                        return f

                    split_width(pe, n, up((0, 1)))
                    with pe.If(i + 1 < n_items):
                        pe.wait_ge(s_ye, 4 * i + 1)
                        index_product(i + 1)
                    split_width(pe, n, up((2, 3)))
                    with pe.If(i + 1 < n_items):
                        x_transposes(i + 1)

                    def down(w):
                        group(i, w, 4)
                        group(i, w, 5)
                        if w == P:
                            pe.sem_inc(s_yt, 4)
                            return
                        with pe.If(i + 1 < n_items):
                            pe.wait_ge(s_xe[0], 2 * i + 4)
                            pe.wait_ge(s_xe[1], 2 * i + 4)
                        pe.wait_ge(s_ye, 4 * i + 1)
                        pe.wait_ge(s_eva, 2 * i + 4)
                        for half in range(2):
                            for b in range(2):
                                for j in range(4):
                                    k = 4 * half + j
                                    last = pe.transpose(psum[4 + 2 * half + b][0:BLK[b], j * P:(j + 1) * P],
                                                        yt[:, k, b * P:b * P + BLK[b]], ident[:])
                                last.then_inc(s_yt, 1)

                    split_width(pe, n, down)

        m = phase()
        ac = [m.take(f"acc{i}", [P, D], F32) for i in range(NT)]
        oo = [m.take(f"out{i}", [P, D], F32) for i in range(NT)]
        gfin = m.take("g_final_row", [P, D], F32)
        dump = m.take("final_dump", [P, D], BF16)
        fs = m.take("final_small", [P, 3 * NT], F32)
        s_fl = [sem(f"acc_landed{i}") for i in range(NT)]
        s_fa2 = sem("final_act")
        s_fr = sem("final_recip")
        s_fo = sem("final_rows")
        s_fs = sem("final_stored")
        s_gf = sem("g_final_landed")
        with nc.Block() as block:
            @block.sync
            def _(sp):
                for i in range(NT):
                    sp.dma_start(ac[i][:], acc_d[i * P:(i + 1) * P, :]).then_inc(s_fl[i], 16)
                    if i == 0:
                        sp.dma_start(gfin[:], g_final.unsqueeze(0).to_broadcast([P, D])).then_inc(s_gf, 16)
                for i in range(NT):
                    sp.wait_ge(s_fo, i + 1)
                    sp.dma_start(out_rows[i * P:(i + 1) * P, :], oo[i][:]).then_inc(s_fs, 16)
                sp.wait_ge(s_fs, 16 * NT)

            @block.scalar
            def _(act):
                for i in range(NT):
                    act.wait_ge(s_fl[i], 16)
                    if i >= 1:
                        act.wait_ge(s_fa2, 2 * i)
                    act.activation(dump[:], ac[i][:], ACT.Square, accum_out=fs[:, i:i + 1]).then_inc(s_fa2, 1)
                    act.wait_ge(s_fa2, 2 * i + 1)
                    act.activation(fs[:, NT + i:NT + i + 1], fs[:, i:i + 1], ACT.Sqrt, bias=epsb[:], scale=1.0 / D).then_inc(s_fa2, 1)

            @block.vector
            def _(dve):
                dve.wait_ge(s_gf, 16)
                for i in range(NT):
                    dve.wait_ge(s_fa2, 2 * i + 2)
                    dve.reciprocal(fs[:, 2 * NT + i:2 * NT + i + 1], fs[:, NT + i:NT + i + 1]).then_inc(s_fr, 1)
                    dve.wait_ge(s_fr, i + 1)
                    dve.scalar_tensor_tensor(out=oo[i][:], in0=ac[i][:], scalar=fs[:, 2 * NT + i:2 * NT + i + 1],
                                             in1=gfin[:], op0=ALU.mult, op1=ALU.mult).then_inc(s_fo, 1)


_INS = ["x", "g_mix", "w_in", "b_forget", "w_pool", "pool_scale", "w_out", "g_ffn", "w_router", "b_router",
        "w_up", "b_up", "w_down", "b_down", "g_final"]


def kernel(**inputs):
    import concourse.bacc as bacc
    from concourse.bass_utils import run_bass_kernel_spmd

    nc = bacc.Bacc("TRN2", target_bir_lowering=False, num_devices=1)
    arrays, args = {}, []
    for name in _INS + ["identity"]:
        a = np.eye(P, dtype=np.float32) if name == "identity" else np.ascontiguousarray(inputs[name])
        arrays[f"in_{name}"] = a
        args.append(nc.dram_tensor(f"in_{name}", a.shape, mybir.dt.from_np(a.dtype), kind="ExternalInput").ap())
    args.append(nc.dram_tensor("out_0", (1, S, D), F32, kind="ExternalOutput").ap())
    build(nc, *args)
    r = run_bass_kernel_spmd(nc, [arrays], core_ids=[0])
    return r.results[0]["out_0"]
```
